# Optimizing a Trainium2 kernel written in Bass

```python
import math
import jax, jax.numpy as jnp
from jax import lax
import numpy as np

D_MODEL = 1024
BATCH = 1
SEQ = 512
DEPTH = 1

CHUNK = 64
MEM_LEN = 256
HEAD_DIM = 64
SB_HEADS = 8
SB_WIDTH = SB_HEADS * HEAD_DIM
POOL_WINDOWS = (2, 4, 8, 16)
POOL_GROUPS = 4
POOL_GROUP_DIM = 64
POOL_WIDTH = POOL_GROUPS * POOL_GROUP_DIM
X_HEADS = 4
X_WIDTH = X_HEADS * HEAD_DIM
N_BRANCH = 3
IN_COLS = 3 * SB_WIDTH + POOL_WIDTH + X_WIDTH + N_BRANCH * D_MODEL
Q_BLOCK = 128
N_GROUPS = 4
EXPERTS_PER_GROUP = 4
N_EXPERTS = N_GROUPS * EXPERTS_PER_GROUP
TOP_K = 2
EXPERT_FF = 512
EPS = 1e-6

kernel_name = "stickbreak_pool_memxattn_hiermoe_trunk"

def rmsnorm(x, g):
    xf = x.astype(jnp.float32)
    y = xf * lax.rsqrt(jnp.mean(xf * xf, axis=-1, keepdims=True) + EPS)
    return (y * g.astype(jnp.float32)).astype(x.dtype)

def stick_breaking_attention(q, k, v):
    B, H, S, Dh = q.shape
    nb = S // Q_BLOCK
    scale = Dh ** -0.5
    qb = q.reshape(B, H, nb, Q_BLOCK, Dh).transpose(2, 0, 1, 3, 4)
    key_pos = jnp.arange(S)

    def block(args):
        qi, i = args
        z = jnp.einsum('bhqd,bhkd->bhqk', qi, k).astype(jnp.float32) * scale
        q_pos = i * Q_BLOCK + jnp.arange(Q_BLOCK)
        strict = key_pos[None, :] < q_pos[:, None]
        log_1m = jnp.where(strict, jax.nn.log_sigmoid(-z), 0.0)
        tail = lax.cumsum(log_1m, axis=3, reverse=True) - log_1m
        a = jnp.where(strict, jnp.exp(jax.nn.log_sigmoid(z) + tail), 0.0)
        return jnp.einsum('bhqk,bhkd->bhqd', a.astype(v.dtype), v)

    out = lax.map(block, (qb, jnp.arange(nb)))
    return out.transpose(1, 2, 0, 3, 4).reshape(B, H, S, Dh)

def multiscale_pool(u, w_pool, pool_scale):
    B, S, _ = u.shape
    ug = u.reshape(B, S, POOL_GROUPS, POOL_GROUP_DIM)
    pos = jnp.arange(1, S + 1, dtype=jnp.float32)
    outs = []
    for g, w in enumerate(POOL_WINDOWS):
        ch = ug[:, :, g].astype(jnp.float32)
        c = jnp.cumsum(ch, axis=1)
        c_lag = jnp.pad(c, ((0, 0), (w, 0), (0, 0)))[:, :S]
        mean = (c - c_lag) / jnp.minimum(pos, w)[None, :, None]
        outs.append(mean - ch)
    d = jnp.stack(outs, axis=2).astype(u.dtype)
    y = jnp.einsum('bsgc,gcd->bsgd', d, w_pool)
    return y.reshape(B, S, POOL_WIDTH) * pool_scale

def memory_cross_attention(qx, mem_n, w_kv_mem):
    B, S, _ = qx.shape
    M = mem_n.shape[1]
    q = qx.reshape(B, S, X_HEADS, HEAD_DIM)
    kv = mem_n @ w_kv_mem
    k = kv[..., :X_WIDTH].reshape(B, M, X_HEADS, HEAD_DIM)
    v = kv[..., X_WIDTH:].reshape(B, M, X_HEADS, HEAD_DIM)
    s = jnp.einsum('bqhd,bmhd->bhqm', q, k).astype(jnp.float32) * (HEAD_DIM ** -0.5)
    p = jax.nn.softmax(s, axis=-1).astype(v.dtype)
    o = jnp.einsum('bhqm,bmhd->bqhd', p, v)
    return o.reshape(B, S, X_WIDTH)

def hybrid_mixer(h, mem_n, w_in, w_pool, pool_scale, w_kv_mem, w_up_sb, w_up_pool, w_up_x, w_out):
    B, S, _ = h.shape
    z = h @ w_in
    o = 0
    q = z[..., o:o + SB_WIDTH]; o += SB_WIDTH
    k = z[..., o:o + SB_WIDTH]; o += SB_WIDTH
    v = z[..., o:o + SB_WIDTH]; o += SB_WIDTH
    u = z[..., o:o + POOL_WIDTH]; o += POOL_WIDTH
    qx = z[..., o:o + X_WIDTH]; o += X_WIDTH
    g = z[..., o:o + N_BRANCH * D_MODEL]

    def heads(t):
        return t.reshape(B, S, SB_HEADS, HEAD_DIM).transpose(0, 2, 1, 3)

    sb = stick_breaking_attention(heads(q), heads(k), heads(v))
    sb = sb.transpose(0, 2, 1, 3).reshape(B, S, SB_WIDTH)
    pl = multiscale_pool(u, w_pool, pool_scale)
    xa = memory_cross_attention(qx, mem_n, w_kv_mem)

    gates = jax.nn.sigmoid(g.astype(jnp.float32)).astype(h.dtype).reshape(B, S, N_BRANCH, D_MODEL)
    merged = (gates[:, :, 0] * (sb @ w_up_sb)
              + gates[:, :, 1] * (pl @ w_up_pool)
              + gates[:, :, 2] * (xa @ w_up_x))
    return merged @ w_out

def hierarchical_moe(h, w_group, b_group, w_router, b_router, w_gate, w_up, w_down):
    B, S, D = h.shape
    t = h.reshape(-1, D)
    T = t.shape[0]
    gl = (t @ w_group).astype(jnp.float32) + b_group.astype(jnp.float32)
    gp = jax.nn.softmax(gl, axis=-1)
    g_idx = jnp.argmax(gl, axis=-1)
    g_prob = jnp.take_along_axis(gp, g_idx[:, None], axis=1)[:, 0]
    el = ((t @ w_router).astype(jnp.float32) + b_router.astype(jnp.float32)).reshape(T, N_GROUPS, EXPERTS_PER_GROUP)
    el_sel = jnp.take_along_axis(el, g_idx[:, None, None], axis=1)[:, 0]
    top_v, top_i = lax.top_k(el_sel, TOP_K)
    wts = jax.nn.softmax(top_v, axis=-1) * g_prob[:, None]
    e_idx = g_idx[:, None] * EXPERTS_PER_GROUP + top_i
    gate = jnp.sum(jax.nn.one_hot(e_idx, N_EXPERTS, dtype=jnp.float32) * wts[..., None], axis=1)
    gate = gate.astype(t.dtype)
    out = jnp.zeros_like(t)
    for e in range(N_EXPERTS):
        a = jax.nn.silu(t @ w_gate[e]) * (t @ w_up[e])
        out = out + gate[:, e:e + 1] * (a @ w_down[e])
    return out.reshape(B, S, D)

def setup_inputs(seed: int = 0) -> dict:
    key = jax.random.key(seed)
    ks = jax.random.split(key, 24)
    f = jnp.float32
    L, D = DEPTH, D_MODEL

    def nrm(k, shape, fan_in):
        return jax.random.normal(k, shape, f) * (fan_in ** -0.5)

    def gain(k, shape):
        return 1.0 + 0.02 * jax.random.normal(k, shape, f)

    return {
        "x": jax.random.normal(ks[0], (BATCH, SEQ, D), f),
        "mem": jax.random.normal(ks[1], (BATCH, MEM_LEN, D), f),
        "norm_mix": gain(ks[2], (L, D)),
        "norm_mem": gain(ks[3], (L, D)),
        "w_in": nrm(ks[4], (L, D, IN_COLS), D),
        "w_pool": nrm(ks[5], (L, POOL_GROUPS, POOL_GROUP_DIM, POOL_GROUP_DIM), POOL_GROUP_DIM),
        "pool_scale": gain(ks[6], (L, POOL_WIDTH)),
        "w_kv_mem": nrm(ks[7], (L, D, 2 * X_WIDTH), D),
        "w_up_sb": nrm(ks[8], (L, SB_WIDTH, D), SB_WIDTH),
        "w_up_pool": nrm(ks[9], (L, POOL_WIDTH, D), POOL_WIDTH),
        "w_up_x": nrm(ks[10], (L, X_WIDTH, D), X_WIDTH),
        "w_out": nrm(ks[11], (L, D, D), D),
        "norm_ffn": gain(ks[12], (L, D)),
        "w_group": nrm(ks[13], (L, D, N_GROUPS), D),
        "b_group": 0.01 * jax.random.normal(ks[14], (L, N_GROUPS), f),
        "w_router": nrm(ks[15], (L, D, N_EXPERTS), D),
        "b_router": 0.01 * jax.random.normal(ks[16], (L, N_EXPERTS), f),
        "w_gate": nrm(ks[17], (L, N_EXPERTS, D, EXPERT_FF), D),
        "w_up": nrm(ks[18], (L, N_EXPERTS, D, EXPERT_FF), D),
        "w_down": nrm(ks[19], (L, N_EXPERTS, EXPERT_FF, D), EXPERT_FF),
        "norm_final": gain(ks[20], (D,)),
    }

def reference(x, mem, norm_mix, norm_mem, w_in, w_pool, pool_scale, w_kv_mem, w_up_sb, w_up_pool,
              w_up_x, w_out, norm_ffn, w_group, b_group, w_router, b_router, w_gate, w_up, w_down,
              norm_final):
    for l in range(DEPTH):
        h = rmsnorm(x, norm_mix[l])
        mem_n = rmsnorm(mem, norm_mem[l])
        x = x + hybrid_mixer(h, mem_n, w_in[l], w_pool[l], pool_scale[l], w_kv_mem[l],
                             w_up_sb[l], w_up_pool[l], w_up_x[l], w_out[l])
        h = rmsnorm(x, norm_ffn[l])
        x = x + hierarchical_moe(h, w_group[l], b_group[l], w_router[l], b_router[l],
                                 w_gate[l], w_up[l], w_down[l])
    return rmsnorm(x, norm_final)


_drawn_inputs = setup_inputs


def setup_inputs(seed=0):
    import zlib

    import numpy as np

    out = dict(_drawn_inputs(seed))
    spreads = {}
    factors = {'norm_mix': 2.848,
     'norm_mem': 8.0,
     'pool_scale': 11.289,
     'b_group': 35.248,
     'b_router': 52.688,
     'norm_final': 8.689,
     'norm_ffn': 8.0}
    for name, (base, spread) in spreads.items():
        noise = np.random.default_rng([zlib.crc32(name.encode()), seed]).standard_normal(out[name].shape)
        drawn = base * np.exp(spread * noise) if base else spread * noise
        out[name] = __import__('jax').numpy.asarray(drawn.astype(out[name].dtype))
    for name, factor in factors.items():
        out[name] = (out[name] * factor).astype(out[name].dtype)
    return out
```

```python
from contextlib import ExitStack

import concourse.bass as bass
from concourse import mybir

F32 = mybir.dt.float32
F32R = mybir.dt.float32r
BF16 = mybir.dt.bfloat16
I32 = mybir.dt.int32
U32 = mybir.dt.uint32
ALU = mybir.AluOpType
ACT = mybir.ActivationFunctionType
AX_X = mybir.AxisListType.X

P = 128
EPS = 1e-6
BIG = 1e30
NEG = -float(2 ** 100)

D = 1024
S = 512
MEM = 256
DH = 64
HEADS = 8
XHEADS = 4
SBW = 512
PW = 256
XW = 256
NG, EPG, NE, FF = 4, 4, 16, 512
KD = D // P
TB = S // P
MB = MEM // P
COL_K, COL_V, COL_U, COL_QX, COL_G = 512, 1024, 1536, 1792, 2048
SCALE = DH ** -0.5

OVER = (2 * S - 1) // P
TILES = NE + OVER
SLOT_TILES = TILES + 1

CW = 2048
SPLIT = 3
RAW = 3
RAW_MOE = 6
FULL = 64
C_KM, C_VM, C_QX, C_U, C_V, C_PAIR = 0, 1, 2, 3, 4, 6
C_MERGE = C_PAIR + HEADS // 2
PER_DP = 6
C_OUT = C_MERGE + PER_DP * (KD // 2)
C_MOE = C_OUT + 4
PER_E = 6
C_OVER = C_MOE + PER_E * NE
assert C_MOE % 2 == 0 and PER_DP % SPLIT == 0 and PER_E % SPLIT == 0

ZOFF = {0: 0, 1: 512, 3: 896, 2: 1024}
ZN = {sb: S - P * sb for sb in range(TB)}
ZW = 1280


def stage_map(base):
    at = {}
    o = base
    for name, size in (("const", 9216), ("ring_hi", 4 * CW * SPLIT), ("ring_lo", 4 * CW * SPLIT),
                       ("raw", 4 * CW * RAW), ("m", 98304), ("t", 30720)):
        at[name] = o
        o += size
    at["end"] = o
    return at


def build_trunk(nc, x, mem, norm_mix, norm_mem, w_in, w_pool, pool_scale, w_kv_mem, w_up_sb,
                w_up_pool, w_up_x, w_out, norm_ffn, w_group, b_group, w_router, b_router,
                w_gate, w_up, w_down, norm_final, out):
    base = (nc.sbuf_base + 63) // 64 * 64
    at = stage_map(base)
    assert at["end"] <= nc.sbuf_usable_end, at

    cursor = {}

    def sb(name, shape, dt, region, offset=None):
        size = 1
        for n in shape[1:]:
            size *= n
        size *= 2 if dt == BF16 else 4
        if offset is None:
            offset = cursor.get(region, 0)
            cursor[region] = offset + (size + 31) // 32 * 32
        return nc.alloc_sbuf_tensor_at(name, shape, dt, offset=at[region] + offset)

    KB = 1024
    ident = sb("ident", [P, P], F32, "const")
    identb = sb("identb", [P, P], BF16, "const")
    negmask = sb("negmask", [P, P], BF16, "const")
    tri_f = sb("tri_f", [P, P], F32, "const")
    negtri = sb("negtri", [P, P], F32R, "const")
    negones = sb("negones", [P, P], F32R, "const")
    rank_tri = sb("rank_tri", [P, P], BF16, "const")
    ones_b = sb("ones_b", [P, P], BF16, "const")
    gain_rows = sb("gain_rows", [2 * KD + 2, P], F32, "const")
    gains = sb("gains", [P, 2 * KD + 2], F32, "const")
    wr = sb("wr", [P, KD, NG + NE], F32, "const")
    bias_bc = sb("bias_bc", [P, NG + NE], F32, "const")
    pos = sb("pos", [P, 16], F32, "const")
    inv_n = sb("inv_n", [P, 2, 16], F32, "const")
    wp = sb("wp", [P, 2, P], F32, "const")
    ss = sb("ss", [P, 16], F32, "const")
    rstd = sb("rstd", [P, 16], F32, "const")
    std = sb("std", [P, 16], F32, "const")
    ms = sb("ms", [P, 16], F32, "const")
    eps_c = sb("eps_c", [P, 1], F32, "const")
    nmx = sb("nmx", [P, 2, 8], F32, "const")
    den = sb("den", [P, 2, 8], F32, "const")
    rden = sb("rden", [P, 2, 8], F32, "const")
    jm = sb("jm", [P, NE], F32, "const")
    e128 = sb("e128", [P, NE], F32, "const")
    wts = sb("wts", [P, 2, TB], F32, "const")
    slot_u = sb("slot_u", [P, 2, TB], I32, "const")
    tab = sb("tab", [P, 8], I32, "const")
    zeros = sb("zeros", [P, 512], F32, "const")
    lgs = sb("lgs", [P, TB, NG + NE], F32, "const")
    ex = sb("ex", [P, TB, 8], F32, "const")
    sm = [sb(f"sm{i}", [P, TB], F32, "const") for i in range(8)]
    assert cursor["const"] <= at["ring_hi"] - at["const"], cursor

    ring_hi = sb("ring_hi", [P, SPLIT, CW], F32R, "ring_hi", 0)
    ring_lo = sb("ring_lo", [P, SPLIT, CW], F32R, "ring_lo", 0)
    raw_a = sb("raw_a", [P, RAW, CW], F32, "raw", 0)

    hT_hi = sb("hT_hi", [P, KD, S], F32R, "m", 0)
    hT_lo = sb("hT_lo", [P, KD, S], F32R, "m", 16 * KB)
    v_hi = sb("v_hi", [P, TB, SBW], F32R, "m", 32 * KB)
    v_lo = sb("v_lo", [P, TB, SBW], F32R, "m", 40 * KB)
    q_hi = sb("q_hi", [P, 2, S], F32R, "m", 48 * KB)
    q_lo = sb("q_lo", [P, 2, S], F32R, "m", 52 * KB)
    k_hi = sb("k_hi", [P, 2, S], F32R, "m", 56 * KB)
    k_lo = sb("k_lo", [P, 2, S], F32R, "m", 60 * KB)
    sbT_hi = sb("sbT_hi", [P, 4, S], F32R, "m", 64 * KB)
    sbT_lo = sb("sbT_lo", [P, 4, S], F32R, "m", 72 * KB)
    plT_hi = sb("plT_hi", [P, 2, S], F32R, "m", 80 * KB)
    plT_lo = sb("plT_lo", [P, 2, S], F32R, "m", 84 * KB)
    xaT_hi = sb("xaT_hi", [P, 2, S], F32R, "m", 88 * KB)
    xaT_lo = sb("xaT_lo", [P, 2, S], F32R, "m", 92 * KB)
    memT_hi = sb("memT_hi", [P, KD, MEM], F32R, "m", 64 * KB)
    memT_lo = sb("memT_lo", [P, KD, MEM], F32R, "m", 72 * KB)
    pT_hi = sb("pT_hi", [P, 4, S], F32R, "m", 64 * KB)
    pT_lo = sb("pT_lo", [P, 4, S], F32R, "m", 72 * KB)
    mgT_hi = sb("mgT_hi", [P, KD, S], F32R, "m", 32 * KB)
    mgT_lo = sb("mgT_lo", [P, KD, S], F32R, "m", 48 * KB)
    xn = sb("xn", [P, TB, D], F32, "t", 0)
    memn = sb("memn", [P, MB, D], F32, "t", 16 * KB)
    junk = sb("junk", [P, D], F32, "t", 24 * KB)
    qx_hi = sb("qx_hi", [P, 2, S], F32R, "t", 0)
    qx_lo = sb("qx_lo", [P, 2, S], F32R, "t", 4 * KB)
    km_hi = sb("km_hi", [P, 2, MEM], F32R, "t", 8 * KB)
    km_lo = sb("km_lo", [P, 2, MEM], F32R, "t", 10 * KB)
    vm_hi = sb("vm_hi", [P, MB, XW], F32R, "t", 12 * KB)
    vm_lo = sb("vm_lo", [P, MB, XW], F32R, "t", 14 * KB)
    U0 = 16
    pool_u = sb("pool_u", [P, 2, U0 + S], F32, "t", 16 * KB)
    pool_a = sb("pool_a", [P, 2, U0 + S], F32, "t", 16 * KB + 4224)
    pool_b = sb("pool_b", [P, 2, U0 + S], F32, "t", 16 * KB + 8448)
    probs = sb("probs", [P, 8, MEM], F32, "t", 16 * KB)
    soft = sb("soft", [P, ZW], F32, "t", 0)
    attn = sb("attn", [P, ZW], F32, "t", 5 * KB)
    soft_hi = sb("soft_hi", [P, ZW], F32R, "t", 10 * KB)
    soft_lo = sb("soft_lo", [P, ZW], F32R, "t", 15 * KB)
    attn_hi = sb("attn_hi", [P, ZW], F32R, "t", 20 * KB)
    attn_lo = sb("attn_lo", [P, ZW], F32R, "t", 25 * KB)
    sig = sb("sig", [P, 3, 2, S], F32, "t", 0)
    merged = sb("merged", [P, 2, S], F32, "t", 12 * KB)
    branch = sb("branch", [P, 2, S], F32, "t", 16 * KB)
    gffn_bc = sb("gffn_bc", [P, D], F32, "t", 24 * KB)
    x2 = sb("x2", [P, TB, D], F32, "m", 0)
    h2 = sb("h2", [P, TB, D], F32, "m", 16 * KB)
    h2T = sb("h2T", [P, KD, S], F32, "t", 0)
    rt = [sb(f"rt{i}", [P, TB, NE], F32, "t", 16 * KB + 256 * i) for i in range(16)]
    onehot_b = sb("onehot_b", [P, TB, NE], BF16, "t", 20 * KB)
    pre = [sb(f"pre{i}", [P, 8 + NE], F32, "t", 20 * KB + 256 + 96 * i) for i in range(2)]
    cmp_t = sb("cmp_t", [P, OVER, NE], F32, "t", 21 * KB)
    raw_b = sb("raw_b", [P, RAW_MOE - RAW, CW], F32, "m", 32 * KB)
    xe = sb("xe", [P, D], F32, "m", 56 * KB)
    xT_hi = sb("xT_hi", [P, D], F32R, "m", 60 * KB)
    xT_lo = sb("xT_lo", [P, D], F32R, "m", 64 * KB)
    silu_g = sb("silu_g", [P, FF], F32, "m", 68 * KB)
    act_e = sb("act_e", [P, FF], F32, "m", 70 * KB)
    aT_hi = sb("aT_hi", [P, FF], F32R, "m", 72 * KB)
    aT_lo = sb("aT_lo", [P, FF], F32R, "m", 74 * KB)
    ye = sb("ye", [P, D], F32, "m", 76 * KB)
    y1 = sb("y1", [P, 2, D], F32, "m", 16 * KB)
    y2 = sb("y2", [P, 2, D], F32, "m", 80 * KB)
    junk2 = sb("junk2", [P, D], F32, "m", 88 * KB)
    gfin_bc = sb("gfin_bc", [P, D], F32, "m", 92 * KB)

    ps = nc.alloc_psum_tensor("ps", [P, 8 * 512], F32)

    def bank(b, n=1):
        return ps[:, 512 * b:512 * (b + n)]

    x_slots = nc.dram_tensor("x_slots", [SLOT_TILES * P, D], F32, kind="Internal").ap()
    y_slots = nc.dram_tensor("y_slots", [TILES * P, D], F32, kind="Internal").ap()

    ctx = ExitStack()
    with ctx:
        sems = {}

        def sem(name):
            sems[name] = ctx.enter_context(nc.semaphore(name))
            return sems[name]

        consts_ready = sem("consts_ready")
        consts_mem = sem("consts_mem")
        gain_in = sem("gain_in")
        mem_in = sem("mem_in")
        sp_free = sem("sp_free")
        x_in = [sem(f"x_in{t}") for t in range(TB)]
        small_in = sem("small_in")
        raw_full = [sem(f"raw_full{s}") for s in range(RAW_MOE)]
        hi_ready = sem("hi_ready")
        lo_ready = sem("lo_ready")
        chunk_used = sem("chunk_used")
        act_c = sem("act_c")
        dve_c = sem("dve_c")
        consts_r = sem("consts_r")
        ss_ready = sem("ss_ready")
        std_ready = sem("std_ready")
        xn_ready = sem("xn_ready")
        gains_ps = sem("gains_ps")
        gains_ready = sem("gains_ready")
        memT_ps = sem("memT_ps")
        memT_h = sem("memT_h")
        memT_l = sem("memT_l")
        hT_ps = sem("hT_ps")
        hT_h = sem("hT_h")
        hT_l = sem("hT_l")
        proj_h = sem("proj_h")
        proj_l = sem("proj_l")
        pool_d = sem("pool_d")
        pool_ps = sem("pool_ps")
        pool_h = sem("pool_h")
        pool_l = sem("pool_l")
        q_ps = sem("q_ps")
        qk_h = sem("qk_h")
        qk_l = sem("qk_l")
        xs_ps = sem("xs_ps")
        xs_max = sem("xs_max")
        xs_exp = sem("xs_exp")
        xs_norm = sem("xs_norm")
        xt_ps = sem("xt_ps")
        xt_h = sem("xt_h")
        xt_l = sem("xt_l")
        xo_ps = sem("xo_ps")
        xo_h = sem("xo_h")
        xo_l = sem("xo_l")
        z_ps = sem("z_ps")
        z_abs = sem("z_abs")
        z_ln = sem("z_ln")
        z_soft = sem("z_soft")
        soft_h = sem("soft_h")
        soft_l = sem("soft_l")
        tail_ps = sem("tail_ps")
        a_exp = sem("a_exp")
        a_h = sem("a_h")
        a_l = sem("a_l")
        av_ps = sem("av_ps")
        av_h = sem("av_h")
        av_l = sem("av_l")
        g_sig = sem("g_sig")
        b_used = sem("b_used")
        b_add = sem("b_add")
        mg_ready = sem("mg_ready")
        mg_h = sem("mg_h")
        mg_l = sem("mg_l")
        xres_in = sem("xres_in")
        x2_ready = sem("x2_ready")
        gffn_in = sem("gffn_in")
        gfin_in = sem("gfin_in")
        h2_ready = sem("h2_ready")
        h2T_ps = sem("h2T_ps")
        h2T_a = sem("h2T_a")
        h2T_v = sem("h2T_v")
        lg_ps = sem("lg_ps")
        r_max = sem("r_max")
        r_exp = sem("r_exp")
        onehot_ready = sem("onehot_ready")
        rank_ps = sem("rank_ps")
        route_ready = sem("route_ready")
        zero_filled = sem("zero_filled")
        scattered = sem("scattered")
        xe_in = sem("xe_in")
        xe_ps = sem("xe_ps")
        xe_h = sem("xe_h")
        xe_l = sem("xe_l")
        silu_ready = sem("silu_ready")
        act_ready = sem("act_ready")
        at_ps = sem("at_ps")
        at_h = sem("at_h")
        at_l = sem("at_l")
        y_a = sem("y_a")
        y_v = sem("y_v")
        y_out = sem("y_out")
        yg_in = [sem("yg_in0"), sem("yg_in1")]
        comb_ready = sem("comb_ready")
        res_ready = sem("res_ready")
        out_done = sem("out_done")

        block = ctx.enter_context(nc.Block())

        def raw_slot(c):
            c0 = c[0]
            if c0 < C_MOE:
                return raw_a[:, c0 % RAW, :], raw_full[c0 % RAW]
            s = (c0 - C_MOE) % RAW_MOE
            return (raw_a[:, s, :] if s < RAW else raw_b[:, s - RAW, :]), raw_full[s]

        def raw_count(c):
            c0, i, per = c
            if c0 < C_MOE:
                n = c0 // RAW + 1
                return FULL * n if i is None else FULL * n + i * (FULL * (per // RAW))
            m = c0 - C_MOE
            s = m % RAW_MOE
            before = len(range(s, C_MOE, RAW)) if s < RAW else 0
            n = before + m // RAW_MOE + 1
            return FULL * n if i is None else FULL * n + i * (FULL * (per // RAW_MOE))

        def upto(c, less=0):
            c0, i, per = c
            n = c0 + 1 - less
            return n if i is None else n + i * per

        def split_hi(act, c, width=CW):
            buf, full = raw_slot(c)
            act.wait_ge(full, raw_count(c))
            if c[0] >= SPLIT or c[1] is not None:
                act.wait_ge(chunk_used, upto(c, SPLIT))
            act.activation(ring_hi[:, c[0] % SPLIT, 0:width], buf[:, 0:width], ACT.Copy).then_inc(hi_ready, 1)

        def split_lo(dve, c, width=CW):
            buf, _ = raw_slot(c)
            s = c[0] % SPLIT
            dve.wait_ge(hi_ready, upto(c))
            dve.tensor_tensor(ring_lo[:, s, 0:width], buf[:, 0:width],
                              ring_hi[:, s, 0:width].bitcast(F32), ALU.subtract).then_inc(lo_ready, 1)

        def K(c0, i=None, per=0):
            return (c0, i, per)

        def after(eng, c):
            eng.wait_ge(chunk_used, upto(c))

        def width_of(c0):
            if C_MERGE <= c0 < C_OUT:
                return (CW, CW, CW, CW // 2, CW // 4, CW // 4)[(c0 - C_MERGE) % PER_DP]
            return CW

        def three(pe, out_ap, l_hi, l_lo, r_hi, r_lo, start, stop):
            pe.matmul(out_ap, l_hi, r_hi, start=start, stop=False, skip_group_check=True)
            pe.matmul(out_ap, l_hi, r_lo, start=False, stop=False, skip_group_check=True)
            return pe.matmul(out_ap, l_lo, r_hi, start=False, stop=stop, skip_group_check=True)

        @block.sync
        def _(sp):
            sp.dma_start(gain_rows[0:KD, :], norm_mix[0].rearrange("(k p) -> k p", p=P)).then_inc(gain_in, 16)
            sp.dma_start(gain_rows[KD:2 * KD, :], norm_mem[0].rearrange("(k p) -> k p", p=P)).then_inc(gain_in, 16)
            sp.dma_start(gain_rows[2 * KD:2 * KD + 2, :], pool_scale[0].rearrange("(k p) -> k p", p=P)).then_inc(gain_in, 16)
            sp.dma_start(memn[:, :, :], mem[0].rearrange("(b p) d -> p b d", p=P)).then_inc(mem_in, 16)

            def load(c, pieces):
                buf, full = raw_slot(c)
                for (a, b, shape), src in pieces:
                    dst = buf[:, a:b].rearrange("p (k n) -> p k n", k=shape)
                    sp.dma_start(dst, src).then_inc(full, FULL // len(pieces))

            def rows(w, k0, k1, c0, c1):
                return w[k0 * P:k1 * P, c0:c1].rearrange("(k p) n -> p k n", p=P)

            win = w_in[0]
            wkv = w_kv_mem[0]
            load(K(C_KM), [((0, CW, KD), rows(wkv, 0, KD, 0, XW))])
            for t in range(TB):
                sp.dma_start(xn[:, t, :], x[0, t * P:(t + 1) * P, :]).then_inc(x_in[t], 16)
            load(K(C_VM), [((0, CW, KD), rows(wkv, 0, KD, XW, 2 * XW))])
            load(K(C_QX), [((0, CW, KD), rows(win, 0, KD, COL_QX, COL_QX + 256))])
            for i, c0 in ((C_U, COL_U),):
                sp.wait_ge(lo_ready, i - RAW + 1)
                load(K(i), [((0, CW, KD), rows(win, 0, KD, c0, c0 + 256))])
            for kh in range(2):
                sp.wait_ge(lo_ready, C_V + kh - RAW + 1)
                load(K(C_V + kh), [((0, CW, 4), rows(win, 4 * kh, 4 * kh + 4, COL_V, COL_V + SBW))])
            for pr in range(HEADS // 2):
                sp.wait_ge(lo_ready, C_PAIR + pr - RAW + 1)
                load(K(C_PAIR + pr), [((0, 1024, KD), rows(win, 0, KD, pr * P, pr * P + P)),
                                      ((1024, 2048, KD), rows(win, 0, KD, COL_K + pr * P, COL_K + pr * P + P))])
            with sp.Fori(0, KD // 2) as dp:
                branch_col = sp.snap(dp * 256)
                for g in range(3):
                    c = K(C_MERGE + g, dp, PER_DP)
                    sp.wait_ge(lo_ready, upto(c, RAW))
                    col = COL_G + g * D
                    load(c, [((0, CW, KD), win[:, bass.ds(dp * 256 + col, 256)].rearrange("(k p) n -> p k n", p=P))])
                for j, (w, kk) in enumerate(((w_up_sb, 4), (w_up_pool, 2), (w_up_x, 2))):
                    c = K(C_MERGE + 3 + j, dp, PER_DP)
                    sp.wait_ge(lo_ready, upto(c, RAW))
                    sp.sem_inc(sp_free, 1)
                    load(c, [((0, kk * 256, kk), w[0][:, bass.ds(branch_col, 256)].rearrange("(k p) n -> p k n", p=P))])
            after(sp, K(C_OUT - 4))
            sp.dma_start(x2[:, :, :], x[0].rearrange("(t p) d -> p t d", p=P)).then_inc(xres_in, 16)
            for i in range(4):
                half, kh = divmod(i, 2)
                sp.wait_ge(lo_ready, C_OUT + i - RAW + 1)
                load(K(C_OUT + i), [((0, CW, 4), rows(w_out[0], 4 * kh, 4 * kh + 4, half * 512, half * 512 + 512))])

            def expert_in(c, i, e):
                k0 = 2 * i * P
                load(c, [((0, CW // 2, 2), w_gate[0, e, k0:k0 + 2 * P, :].rearrange("(k p) n -> p k n", p=P)),
                         ((CW // 2, CW, 2), w_up[0, e, k0:k0 + 2 * P, :].rearrange("(k p) n -> p k n", p=P))])

            def expert_out(c, i, e):
                k0 = 2 * i * P
                load(c, [((0, CW, 2), w_down[0, e, k0:k0 + 2 * P, :].rearrange("(k p) n -> p k n", p=P))])

            for i in range(4):
                s = i % RAW_MOE
                if s < RAW:
                    last = max(c for c in range(C_MOE) if c % RAW == s)
                    sp.wait_ge(lo_ready, last + 1)
                else:
                    after(sp, K(C_OUT + 3))
                expert_in(K(C_MOE + i), i, 0)
            for i in range(2):
                c = K(C_MOE + 4 + i)
                after(sp, K(C_OUT + 3))
                expert_in(c, i, 1)
            for i in range(2, 4):
                c = K(C_MOE + 4 + i)
                sp.wait_ge(lo_ready, upto(c, RAW_MOE))
                expert_in(c, i, 1)
            for i in range(2):
                c = K(C_MOE + 8 + i)
                sp.wait_ge(lo_ready, upto(c, RAW_MOE))
                expert_out(c, i, 0)
            with sp.Fori(0, NE - 2) as j:
                for i in range(4):
                    c = K(C_MOE + 10 + i, j, PER_E)
                    sp.wait_ge(lo_ready, upto(c, RAW_MOE))
                    expert_in(c, i, j + 2)
                for i in range(2):
                    c = K(C_MOE + 14 + i, j, PER_E)
                    sp.wait_ge(lo_ready, upto(c, RAW_MOE))
                    expert_out(c, i, j + 1)
            for i in range(2):
                c = K(C_OVER - 2 + i)
                sp.wait_ge(lo_ready, upto(c, RAW_MOE))
                expert_out(c, i, NE - 1)
            sp.wait_ge(route_ready, 1)
            n_over = sp.value_load(tab[0:1, 0:1], min_val=0, max_val=OVER)
            with sp.Fori(0, OVER) as j:
                with sp.If(n_over > j):
                    e = sp.value_load(tab[0:1, bass.ds(j + 1, 1)], min_val=0, max_val=NE - 1)
                    for i in range(4):
                        c = K(C_OVER + i, j, PER_E)
                        sp.wait_ge(lo_ready, upto(c, RAW_MOE))
                        expert_in(c, i, e)
                    for i in range(2):
                        c = K(C_OVER + 4 + i, j, PER_E)
                        sp.wait_ge(lo_ready, upto(c, RAW_MOE))
                        expert_out(c, i, e)
                sp.nop()
            for t in range(TB):
                sp.wait_ge(res_ready, t + 1)
                sp.dma_start(out[0, t * P:(t + 1) * P, :], x2[:, t, :]).then_inc(out_done, 16)
            sp.wait_ge(out_done, 16 * TB)

        @block.gpsimd
        def _(pool):
            n_step = [0]

            def step(ins):
                n_step[0] += 1
                ins.then_inc(consts_mem, 1)
                pool.wait_ge(consts_mem, n_step[0])

            step(pool.memset(eps_c[:, :], EPS))
            step(pool.memset(ident[:, :], 0.0))
            step(pool.affine_select(out=ident[:, :], in_=ident[:, :], compare_op=ALU.not_equal, fill=1.0,
                                    base=0, pattern=[[-1, P]], channel_multiplier=1))
            step(pool.memset(tri_f[:, :], 0.0))
            step(pool.affine_select(out=tri_f[:, :], in_=tri_f[:, :], compare_op=ALU.is_gt, fill=-1.0,
                                    base=0, pattern=[[1, P]], channel_multiplier=-1))
            step(pool.memset(negmask[:, :], 0.0))
            step(pool.affine_select(out=negmask[:, :], in_=negmask[:, :], compare_op=ALU.is_gt, fill=NEG,
                                    base=0, pattern=[[1, P]], channel_multiplier=-1))
            step(pool.memset(rank_tri[:, :], 1.0))
            step(pool.affine_select(out=rank_tri[:, :], in_=rank_tri[:, :], compare_op=ALU.is_gt, fill=0.0,
                                    base=0, pattern=[[1, P]], channel_multiplier=-1))
            step(pool.memset(ones_b[:, :], 1.0))
            step(pool.iota(pos[:, :], pattern=[[1, 16]], base=1, channel_multiplier=0,
                           allow_small_or_imprecise_dtypes=True))
            step(pool.iota(jm[:, :], pattern=[[1, NE]], base=-64, channel_multiplier=0,
                           allow_small_or_imprecise_dtypes=True))
            step(pool.iota(e128[:, :], pattern=[[P, NE]], base=0, channel_multiplier=0,
                           allow_small_or_imprecise_dtypes=True))
            step(pool.memset(wp[:, :, :], 0.0))
            step(pool.memset(zeros[:, :], 0.0))
            pool.sem_inc(consts_ready, 1)
            for g in range(4):
                lo = DH * (g % 2)
                pool.dma_start(wp[lo:lo + DH, g // 2, lo:lo + DH], w_pool[0, g]).then_inc(small_in, 16)
            pool.dma_start(wr[:, :, 0:NG], w_group[0].rearrange("(k p) n -> p k n", p=P)).then_inc(small_in, 16)
            pool.dma_start(wr[:, :, NG:NG + NE], w_router[0].rearrange("(k p) n -> p k n", p=P)).then_inc(small_in, 16)
            pool.dma_start(bias_bc[:, 0:NG], b_group[0:1, :].broadcast_to([P, NG])).then_inc(small_in, 16)
            pool.dma_start(bias_bc[:, NG:NG + NE], b_router[0:1, :].broadcast_to([P, NE])).then_inc(small_in, 16)
            pool.wait_ge(z_ps, 1)
            slots_v = x_slots.rearrange("(p n) (h d) -> p (n h) d", p=P, h=2)
            for n in range(0, 2 * SLOT_TILES, 12):
                pool.dma_start(slots_v[:, n:n + 12, :],
                               zeros[:, :].unsqueeze(1).broadcast_to([P, 12, 512])).then_inc(zero_filled, 16)
            pool.dma_start(y_slots[NE * P:, :].rearrange("(p n) (h d) -> p (n h) d", p=P, h=2),
                           zeros[:, :].unsqueeze(1).broadcast_to([P, 2 * OVER, 512])).then_inc(zero_filled, 16)
            pool.wait_ge(b_used, 3)
            pool.dma_start(gffn_bc[:, :], norm_ffn[0:1, :].broadcast_to([P, D])).then_inc(gffn_in, 16)
            after(pool, K(C_OUT + 1))
            pool.dma_start(gfin_bc[:, :], norm_final.rearrange("(a d) -> a d", a=1).broadcast_to([P, D])).then_inc(gfin_in, 16)
            pool.wait_ge(route_ready, 1)
            pool.wait_ge(zero_filled, 16 * (2 * SLOT_TILES // 12 + 1))
            for r in range(2):
                for t in range(TB):
                    pool.indirect_dma_start(
                        x_slots[:, :], bass.IndirectOffsetOnAxis(slot_u[:, r, t:t + 1].bitcast(U32), 0),
                        h2[:, t, :], None).then_inc(scattered, 16)
            pool.wait_ge(scattered, 16 * 2 * TB)

            def x_load(tile, n):
                pool.wait_ge(xe_ps, n)
                pool.dma_start(xe[:, :], x_slots[bass.ds(tile * P, P), :]).then_inc(xe_in, 16)

            def y_store(tile, n):
                pool.wait_ge(y_a, n)
                pool.wait_ge(y_v, n)
                pool.dma_start(y_slots[bass.ds(tile * P, P), :], ye[:, :]).then_inc(y_out, 16)

            pool.dma_start(xe[:, :], x_slots[0:P, :]).then_inc(xe_in, 16)
            x_load(1, 1)
            with pool.Fori(0, NE - 1) as j:
                x_load(j + 2, j + 2)
                y_store(j, j + 1)
            y_store(NE - 1, NE)
            n_over = pool.value_load(tab[0:1, 0:1], min_val=0, max_val=OVER)
            with pool.Fori(0, OVER) as j:
                with pool.If(n_over > j):
                    x_load(j + NE + 1, j + NE + 1)
                    y_store(j + NE, j + NE + 1)
                    pool.wait_ge(y_out, (j + NE + 1) * 16)
                pool.nop()
            pool.wait_ge(y_out, 16 * NE)
            for t in range(TB):
                if t >= 2:
                    pool.wait_ge(comb_ready, t - 1)
                for r, y in ((0, y1), (1, y2)):
                    pool.indirect_dma_start(
                        y[:, t % 2, :], None, y_slots[:, :],
                        bass.IndirectOffsetOnAxis(slot_u[:, r, t:t + 1].bitcast(U32), 0)).then_inc(yg_in[t % 2], 16)

        @block.scalar
        def _(act):
            def root(cols, n):
                act.wait_ge(ss_ready, n)
                act.activation(std[:, cols], ss[:, cols], ACT.Sqrt, scale=1.0 / D, bias=eps_c[:, :]) \
                   .then_inc(std_ready, cols.stop - cols.start)

            act.wait_ge(mem_in, 16)
            for b in range(MB):
                if b:
                    act.wait_ge(ss_ready, b)
                act.activation(junk[:, :], memn[:, b, :], ACT.Square, accum_out=ss[:, b:b + 1]).then_inc(ss_ready, 1)
            act.wait_ge(consts_ready, 1)
            root(slice(0, MB), MB)
            split_hi(act, K(0))
            for t in range(TB):
                act.wait_ge(x_in[t], 16)
                act.wait_ge(ss_ready, MB + t)
                act.activation(junk[:, :], xn[:, t, :], ACT.Square, accum_out=ss[:, MB + t:MB + t + 1]).then_inc(ss_ready, 1)
            root(slice(MB, MB + TB), MB + TB)
            split_hi(act, K(1))
            act.activation(negtri[:, :], tri_f[:, :], ACT.Copy).then_inc(consts_r, 1)
            act.activation(negones[:, :], ones_b[:, :], ACT.Copy, scale=-1.0).then_inc(consts_r, 1)
            act.activation(identb[:, :], ident[:, :], ACT.Copy).then_inc(consts_r, 1)
            act.wait_ge(gains_ready, 1)
            for b in range(4):
                act.wait_ge(memT_ps, b + 1)
                for k in (2 * b, 2 * b + 1):
                    act.activation(memT_hi[:, k, :], bank(b)[:, (k % 2) * MEM:(k % 2 + 1) * MEM], ACT.Copy,
                                   scale=gains[:, KD + k:KD + k + 1]).then_inc(memT_h, 1)
            for k in range(KD):
                act.wait_ge(hT_ps, k + 1)
                act.activation(hT_hi[:, k, :], bank(4 + k % 4), ACT.Copy,
                               scale=gains[:, k:k + 1]).then_inc(hT_h, 1)

            def proj_hi(n, ahead, dst, src):
                if ahead is not None:
                    split_hi(act, K(ahead))
                if dst is not None:
                    after(act, K((C_KM, C_VM, C_QX, C_U, C_V + 1)[n - 1]))
                    act.activation(dst, src, ACT.Copy).then_inc(proj_h, 1)

            proj_hi(1, C_KM + 2, km_hi[:, :, :], bank(0))
            proj_hi(2, C_VM + 2, vm_hi[:, :, :], bank(1))
            proj_hi(3, C_QX + 2, qx_hi[:, :, :], bank(2, 2))
            proj_hi(4, C_U + 2, None, None)
            proj_hi(5, C_V + 2, v_hi[:, :, :], bank(0, 4))
            split_hi(act, K(C_V + 3))

            def qk_hi(n, b):
                if n % 2:
                    after(act, K(C_PAIR + n // 2))
                else:
                    act.wait_ge(q_ps, n // 2 + 1)
                dst = (k_hi if n % 2 else q_hi)[:, n // 2 % 2, :]
                act.activation(dst, bank(b), ACT.Copy, scale=1.0 if n % 2 else SCALE).then_inc(qk_h, 1)

            def cross_exp(r):
                act.wait_ge(xs_max, r + 1)
                if r == 0:
                    act.wait_ge(pool_ps, 1)
                else:
                    act.wait_ge(xt_ps, r)
                for i in range(8):
                    ins = act.activation(probs[:, i, :], bank(4, 4)[:, i * MEM:(i + 1) * MEM], ACT.Exp,
                                         bias=nmx[:, r, i:i + 1], scale=SCALE, accum_out=den[:, r, i:i + 1])
                ins.then_inc(xs_exp, 1)

            def cross_t(r):
                act.wait_ge(xt_ps, r + 1)
                if r > 0:
                    act.wait_ge(xo_ps, r)
                act.activation(pT_hi[:, :, :], bank(4, 4), ACT.Copy).then_inc(xt_h, 1)

            def cross_o(r):
                act.wait_ge(xo_ps, r + 1)
                for h in range(2):
                    rows = slice(DH * h, DH * h + DH)
                    ins = act.activation(xaT_hi[rows, r, :], bank(h)[rows, :], ACT.Copy)
                ins.then_inc(xo_h, 1)

            act.wait_ge(pool_ps, 1)
            for c in range(2):
                act.activation(plT_hi[:, c, :], bank(c), ACT.Copy,
                               scale=gains[:, 2 * KD + c:2 * KD + c + 1]).then_inc(pool_h, 1)
            cross_exp(0)
            split_hi(act, K(C_PAIR + 2))
            qk_hi(0, 2)
            qk_hi(1, 3)
            cross_t(0)
            split_hi(act, K(C_PAIR + 3))
            qk_hi(2, 2)
            qk_hi(3, 3)
            cross_o(0)
            cross_exp(1)
            cross_t(1)
            cross_o(1)

            for n in range(HEADS + 2):
                z = bank(3 * (n % 2), 3)[:, 0:ZW]
                z_last = bank(3 * ((n + 1) % 2), 3)[:, 0:ZW]
                if n < HEADS:
                    act.wait_ge(z_abs, n + 1)
                    act.activation(soft[:, :], soft[:, :], ACT.Exp, scale=-1.0).then_inc(act_c, 1)
                    act.wait_ge(act_c, n + 1)
                    act.activation(soft[:, :], soft[:, :], ACT.Ln, bias=1.0).then_inc(z_ln, 1)
                if 1 <= n <= HEADS:
                    act.wait_ge(tail_ps, n)
                    if n >= 2:
                        act.wait_ge(a_l, n - 1)
                    act.activation(attn[:, :], z_last, ACT.Exp).then_inc(a_exp, 1)
                if n < HEADS:
                    act.wait_ge(z_soft, n + 1)
                    act.activation(soft_hi[:, :], soft[:, :], ACT.Copy).then_inc(soft_h, 1)
                if n in (2, 4):
                    split_hi(act, K(C_MERGE + (n - 2) // 2))
                if n >= 2:
                    m = n - 2
                    rows = slice(DH * (m % 2), DH * (m % 2) + DH)
                    act.wait_ge(av_ps, m + 1)
                    act.activation(sbT_hi[rows, m // 2, :], bank(7)[rows, :], ACT.Copy).then_inc(av_h, 1)
                if 2 <= n < 6:
                    qk_hi(n + 2, 6)

            with act.Fori(0, KD // 2) as dp:
                for i in range(PER_DP):
                    split_hi(act, K(C_MERGE + i + 2, dp, PER_DP), width_of(C_MERGE + (i + 2) % PER_DP))
                    if i < 3:
                        after(act, K(C_MERGE + i, dp, PER_DP))
                        act.activation(sig[:, i, :, :], bank(2 * i, 2), ACT.Sigmoid).then_inc(g_sig, 1)
                act.wait_ge(mg_ready, dp + 1)
                act.activation(mgT_hi[:, bass.ds(dp * 2, 2), :], merged[:, :, :], ACT.Copy).then_inc(mg_h, 1)
            for i in range(4):
                split_hi(act, K(C_OUT + i + 2))
            split_hi(act, K(C_MOE + 2))

            act.wait_ge(x2_ready, 2)
            for t in range(TB):
                act.wait_ge(ss_ready, MB + TB + t)
                act.activation(junk2[:, :], x2[:, t, :], ACT.Square, accum_out=ss[:, 8 + t:9 + t]).then_inc(ss_ready, 1)
            root(slice(8, 8 + TB), MB + 2 * TB)
            for k in range(0, KD, 2):
                act.wait_ge(h2T_ps, k + 1)
                act.activation(h2T[:, k, :], bank(k % 4), ACT.Copy).then_inc(h2T_a, 1)
            act.wait_ge(r_max, 1)
            act.activation(ex[:, :, 0:5], ex[:, :, 0:5], ACT.Exp).then_inc(r_exp, 1)

            def xe_hi(n):
                act.wait_ge(xe_ps, n)
                act.activation(xT_hi[:, :], bank(2, 2), ACT.Copy).then_inc(xe_h, 1)

            def silu(c):
                after(act, c)
                act.activation(silu_g[:, :], bank(0), ACT.Silu).then_inc(silu_ready, 1)

            def aT_h(n):
                act.wait_ge(at_ps, n)
                act.activation(aT_hi[:, :], bank(4), ACT.Copy).then_inc(at_h, 1)

            def y_half(c, stored):
                after(act, c)
                if stored is not None:
                    act.wait_ge(y_out, stored)
                act.activation(ye[:, 0:512], bank(5), ACT.Copy).then_inc(y_a, 1)

            xe_hi(1)
            for i in range(4):
                if i > 0:
                    split_hi(act, K(C_MOE + i + 2))
            silu(K(C_MOE + 3))
            xe_hi(2)
            for i in range(PER_E):
                split_hi(act, K(C_MOE + 4 + i + 2))
                if i == 1:
                    aT_h(1)
                if i == 3:
                    silu(K(C_MOE + 7))
                    xe_hi(3)
            y_half(K(C_MOE + 9), None)
            with act.Fori(0, NE - 2) as j:
                for i in range(PER_E):
                    if i == 1:
                        pass
                    split_hi(act, K(C_MOE + 10 + i + 2, j, PER_E))
                    if i == 1:
                        aT_h(j + 2)
                    if i == 3:
                        silu(K(C_MOE + 13, j, PER_E))
                        xe_hi(j + 4)
                y_half(K(C_MOE + 15, j, PER_E), (j + 1) * 16)
            aT_h(NE)
            y_half(K(C_OVER - 1), 16 * (NE - 1))
            act.wait_ge(route_ready, 1)
            n_over = act.value_load(tab[0:1, 0:1], min_val=0, max_val=OVER)
            with act.Fori(0, OVER) as j:
                with act.If(n_over > j):
                    for i in range(PER_E):
                        split_hi(act, K(C_OVER + i, j, PER_E))
                    silu(K(C_OVER + 3, j, PER_E))
                    xe_hi(j + NE + 2)
                    aT_h(j + NE + 1)
                    y_half(K(C_OVER + 5, j, PER_E), (j + NE) * 16)
                act.nop()
            for t in range(TB):
                act.wait_ge(comb_ready, t + 1)
                act.wait_ge(ss_ready, MB + 2 * TB + t)
                act.activation(junk2[:, :], x2[:, t, :], ACT.Square, accum_out=ss[:, 12 + t:13 + t]).then_inc(ss_ready, 1)
                root(slice(12 + t, 13 + t), MB + 2 * TB + t + 1)

        @block.tensor
        def _(pe):
            def chunk(c):
                pe.wait_ge(lo_ready, upto(c))
                s = c[0] % SPLIT
                return ring_hi[:, s, :], ring_lo[:, s, :]

            pe.wait_ge(consts_ready, 1)
            pe.wait_ge(gain_in, 48)
            pe.transpose(bank(7)[:, 0:2 * KD + 2], gain_rows[:, :], ident[0:2 * KD + 2, 0:2 * KD + 2]).then_inc(gains_ps, 1)
            for b in range(4):
                if b == 0:
                    pe.wait_ge(xn_ready, MB)
                for k in (2 * b, 2 * b + 1):
                    for m in range(MB):
                        o = (k % 2) * MEM + m * P
                        ins = pe.transpose(bank(b)[:, o:o + P], memn[:, m, k * P:(k + 1) * P], ident[:, :])
                ins.then_inc(memT_ps, 1)
            pe.wait_ge(xn_ready, MB + TB)
            pe.wait_ge(gains_ready, 1)
            for k in range(KD):
                if k >= 4:
                    pe.wait_ge(hT_l, k - 3)
                for t in range(TB):
                    ins = pe.transpose(bank(4 + k % 4)[:, t * P:(t + 1) * P], xn[:, t, k * P:(k + 1) * P], ident[:, :])
                ins.then_inc(hT_ps, 1)

            pe.wait_ge(memT_l, KD)
            wh, wl = chunk(K(C_KM))
            for c in range(2):
                for k in range(KD):
                    o = k * 256 + c * P
                    ins = three(pe, bank(0)[:, c * MEM:(c + 1) * MEM], wh[:, o:o + P], wl[:, o:o + P],
                                memT_hi[:, k, :], memT_lo[:, k, :], k == 0, k == KD - 1)
            ins.then_inc(chunk_used, 1)
            wh, wl = chunk(K(C_VM))
            for m in range(MB):
                for k in range(KD):
                    ins = three(pe, bank(1)[:, m * XW:(m + 1) * XW], memT_hi[:, k, m * P:(m + 1) * P],
                                memT_lo[:, k, m * P:(m + 1) * P], wh[:, k * 256:(k + 1) * 256],
                                wl[:, k * 256:(k + 1) * 256], k == 0, k == KD - 1)
            ins.then_inc(chunk_used, 1)

            def proj(b, wh, wl, o0, step):
                for k in range(KD):
                    o = o0 + k * step
                    ins = three(pe, bank(b), wh[:, o:o + P], wl[:, o:o + P], hT_hi[:, k, :], hT_lo[:, k, :],
                                k == 0, k == KD - 1)
                return ins

            pe.wait_ge(hT_l, KD)
            wh, wl = chunk(K(C_QX))
            proj(2, wh, wl, 0, 256)
            proj(3, wh, wl, P, 256).then_inc(chunk_used, 1)
            wh, wl = chunk(K(C_U))
            proj(4, wh, wl, 0, 256)
            proj(5, wh, wl, P, 256).then_inc(chunk_used, 1)
            pe.wait_ge(proj_l, 3)
            for kh in range(2):
                wh, wl = chunk(K(C_V + kh))
                for kk in range(4):
                    for t in range(TB):
                        k = 4 * kh + kk
                        ins = three(pe, bank(t), hT_hi[:, k, t * P:(t + 1) * P], hT_lo[:, k, t * P:(t + 1) * P],
                                    wh[:, kk * 512:(kk + 1) * 512], wl[:, kk * 512:(kk + 1) * 512],
                                    k == 0, k == KD - 1)
                ins.then_inc(chunk_used, 1)

            def cross_scores(r):
                if r == 0:
                    pe.wait_ge(proj_l, 3)
                    pe.wait_ge(pool_d, 1)
                else:
                    pe.wait_ge(xt_l, r)
                for h in range(2):
                    rows = slice(DH * h, DH * h + DH)
                    for t in range(TB):
                        o = (h * TB + t) * MEM
                        ins = three(pe, bank(4, 4)[:, o:o + MEM], qx_hi[rows, r, t * P:(t + 1) * P],
                                    qx_lo[rows, r, t * P:(t + 1) * P], km_hi[rows, r, :], km_lo[rows, r, :],
                                    True, True)
                ins.then_inc(xs_ps, 1)

            def cross_transpose(r):
                pe.wait_ge(xs_norm, r + 1)
                for h in range(2):
                    for m in range(MB):
                        for t in range(TB):
                            ins = pe.transpose(bank(4 + 2 * h + m)[:, t * P:(t + 1) * P],
                                               probs[:, h * TB + t, m * P:(m + 1) * P], ident[:, :])
                ins.then_inc(xt_ps, 1)

            def cross_out(r):
                pe.wait_ge(xt_l, r + 1)
                pe.wait_ge(pool_l if r == 0 else xo_l, 2 if r == 0 else r)
                for h in range(2):
                    for m in range(MB):
                        ins = three(pe, bank(h), vm_hi[:, m, r * P:(r + 1) * P], vm_lo[:, m, r * P:(r + 1) * P],
                                    pT_hi[:, 2 * h + m, :], pT_lo[:, 2 * h + m, :], m == 0, m == MB - 1)
                ins.then_inc(xo_ps, 1)

            def project_qk(n, b):
                wh, wl = chunk(K(C_PAIR + n // 2))
                if n >= 4:
                    pe.wait_ge(z_ps, n - 2)
                proj(b, wh, wl, 1024 * (n % 2), P).then_inc(chunk_used if n % 2 else q_ps, 1)

            cross_scores(0)
            pe.wait_ge(pool_d, 2)
            pe.wait_ge(proj_l, 4)
            pe.wait_ge(small_in, 16 * 8)
            for c in range(2):
                ins = pe.matmul(bank(c), wp[:, c, :], pool_a[:, c, U0:], start=True, stop=True)
            ins.then_inc(pool_ps, 1)
            project_qk(0, 2)
            project_qk(1, 3)
            cross_transpose(0)
            pe.wait_ge(qk_l, 1)
            project_qk(2, 2)
            pe.wait_ge(qk_l, 2)
            project_qk(3, 3)
            cross_out(0)
            cross_scores(1)
            cross_transpose(1)
            cross_out(1)

            for n in range(HEADS + 2):
                if n < HEADS:
                    rows = slice(DH * (n % 2), DH * (n % 2) + DH)
                    z0 = 3 * (n % 2)
                    pe.wait_ge(qk_l, 2 * (n // 2) + 2)
                    if n == 0:
                        pe.wait_ge(xo_l, 2)
                    if n == 1:
                        pe.wait_ge(xt_l, 2)
                    if n >= 2:
                        pe.wait_ge(a_exp, n - 1)
                    for sbk in (0, 1, 3, 2):
                        keys = slice(sbk * P, sbk * P + P)
                        o, w = ZOFF[sbk], ZN[sbk]
                        first = sbk != 3
                        zz = bank(z0, 3)
                        three(pe, zz[:, o:o + w], k_hi[rows, n // 2 % 2, keys], k_lo[rows, n // 2 % 2, keys],
                              q_hi[rows, n // 2 % 2, sbk * P:], q_lo[rows, n // 2 % 2, sbk * P:], first, False)
                        ins = pe.matmul(zz[:, o:o + P], identb[:, :], negmask[:, :], start=False, stop=True,
                                        skip_group_check=True)
                    ins.then_inc(z_ps, 1)
                if n >= 2:
                    m = n - 2
                    pr = m // 2
                    pe.wait_ge(a_l, m + 1)
                    if m >= 1:
                        pe.wait_ge(av_l, m)
                    for sbk in range(TB):
                        o, w = ZOFF[sbk], ZN[sbk]
                        ins = three(pe, bank(7)[:, sbk * P:], v_hi[:, sbk, pr * P:(pr + 1) * P],
                                    v_lo[:, sbk, pr * P:(pr + 1) * P], attn_hi[:, o:o + w], attn_lo[:, o:o + w],
                                    sbk == 0, sbk == TB - 1)
                    ins.then_inc(av_ps, 1)
                if 1 <= n <= HEADS:
                    z0 = 3 * ((n - 1) % 2)
                    pe.wait_ge(soft_l, n)
                    zz = bank(z0, 3)
                    for sbk in range(TB):
                        for jb in range(sbk, TB):
                            o = ZOFF[sbk] + (jb - sbk) * P
                            j, w = ZOFF[jb], ZN[jb]
                            lhs = negtri if jb == sbk else negones
                            pe.matmul(zz[:, o:o + w], lhs[:, :], soft_hi[:, j:j + w], start=False, stop=False,
                                      skip_group_check=True)
                            ins = pe.matmul(zz[:, o:o + w], lhs[:, :], soft_lo[:, j:j + w], start=False,
                                            stop=jb == TB - 1, skip_group_check=True)
                    ins.then_inc(tail_ps, 1)
                if 2 <= n < 6:
                    if n >= 3:
                        pe.wait_ge(qk_l, n + 2)
                    project_qk(n + 2, 6)

            pe.wait_ge(av_l, HEADS)
            pe.wait_ge(xo_l, 2)
            pe.wait_ge(pool_l, 2)
            branches = ((sbT_hi, sbT_lo, 4), (plT_hi, plT_lo, 2), (xaT_hi, xaT_lo, 2))
            with pe.Fori(0, KD // 2) as dp:
                for g in range(3):
                    pe.wait_ge(b_used, dp * 3 + g + 1)
                    wh, wl = chunk(K(C_MERGE + g, dp, PER_DP))
                    proj(2 * g, wh, wl, 0, 256)
                    proj(2 * g + 1, wh, wl, P, 256).then_inc(chunk_used, 1)
                for j, (bh, bl, kk) in enumerate(branches):
                    pe.wait_ge(g_sig, dp * 3 + j + 1)
                    wh, wl = chunk(K(C_MERGE + 3 + j, dp, PER_DP))
                    for c in range(2):
                        for k in range(kk):
                            o = k * 256 + c * P
                            ins = three(pe, bank(2 * j + c), wh[:, o:o + P], wl[:, o:o + P], bh[:, k, :], bl[:, k, :],
                                        k == 0, k == kk - 1)
                    ins.then_inc(chunk_used, 1)

            pe.wait_ge(mg_l, KD // 2)
            pe.wait_ge(b_used, 3 + 3 * (KD // 2))
            for half in range(2):
                for kh in range(2):
                    wh, wl = chunk(K(C_OUT + 2 * half + kh))
                    for kk in range(4):
                        for t in range(TB):
                            k = 4 * kh + kk
                            ins = three(pe, bank(4 * half + t), mgT_hi[:, k, t * P:(t + 1) * P],
                                        mgT_lo[:, k, t * P:(t + 1) * P], wh[:, kk * 512:(kk + 1) * 512],
                                        wl[:, kk * 512:(kk + 1) * 512], k == 0, k == KD - 1)
                    ins.then_inc(chunk_used, 1)

            pe.wait_ge(x2_ready, 2)
            pe.wait_ge(h2_ready, TB)
            for k in range(KD):
                if k >= 4:
                    if k % 2 == 0:
                        pe.wait_ge(h2T_a, k // 2 - 1)
                    else:
                        pe.wait_ge(h2T_v, k // 2 - 1)
                for t in range(TB):
                    ins = pe.transpose(bank(k % 4)[:, t * P:(t + 1) * P], h2[:, t, k * P:(k + 1) * P], ident[:, :])
                ins.then_inc(h2T_ps, 1)
            pe.wait_ge(h2T_a, KD // 2)
            pe.wait_ge(h2T_v, KD // 2)
            for t in range(TB):
                for k in range(KD):
                    ins = pe.matmul(bank(4)[:, t * (NG + NE):(t + 1) * (NG + NE)], h2T[:, k, t * P:(t + 1) * P],
                                    wr[:, k, :], start=k == 0, stop=k == KD - 1)
            ins.then_inc(lg_ps, 1)
            pe.wait_ge(onehot_ready, 1)
            for t in range(TB):
                for u in range(t + 1):
                    pe.matmul(bank(5)[:, t * NE:(t + 1) * NE], (rank_tri if u == t else ones_b)[:, :],
                              onehot_b[:, u, :], start=u == 0, stop=u == t)
            for u in range(TB):
                ins = pe.matmul(bank(5)[:, TB * NE:(TB + 1) * NE], ones_b[:, :], onehot_b[:, u, :],
                                start=u == 0, stop=u == TB - 1)
            ins.then_inc(rank_ps, 1)

            def x_transpose(n, read):
                pe.wait_ge(xe_in, n * 16)
                if read is not None:
                    pe.wait_ge(xe_l, read)
                for k in range(KD):
                    ins = pe.transpose(bank(2, 2)[:, k * P:(k + 1) * P], xe[:, k * P:(k + 1) * P], ident[:, :])
                ins.then_inc(xe_ps, 1)

            def gate_up(n, c0, i, j, before):
                if i == 0:
                    pe.wait_ge(xe_l, n)
                    if before is not None:
                        pe.wait_ge(act_ready, before)
                wh, wl = chunk(K(c0 + i, j, PER_E))
                for kk in range(2):
                    k = 2 * i + kk
                    for u in range(2):
                        o = u * 1024 + kk * 512
                        ins = three(pe, bank(u), xT_hi[:, k * P:(k + 1) * P], xT_lo[:, k * P:(k + 1) * P],
                                    wh[:, o:o + 512], wl[:, o:o + 512], k == 0, k == KD - 1)
                ins.then_inc(chunk_used, 1)

            def a_transpose(n, read):
                pe.wait_ge(act_ready, n)
                if read is not None:
                    pe.wait_ge(at_l, read)
                for f in range(4):
                    ins = pe.transpose(bank(4)[:, f * P:(f + 1) * P], act_e[:, f * P:(f + 1) * P], ident[:, :])
                ins.then_inc(at_ps, 1)

            def down(n, c0, j, read):
                pe.wait_ge(at_l, n)
                if read is not None:
                    pe.wait_ge(y_a, read)
                    pe.wait_ge(y_v, read)
                for i in range(2):
                    wh, wl = chunk(K(c0 + i, j, PER_E))
                    for kk in range(2):
                        f = 2 * i + kk
                        for half in range(2):
                            o = kk * 1024 + half * 512
                            ins = three(pe, bank(5 + half), aT_hi[:, f * P:(f + 1) * P], aT_lo[:, f * P:(f + 1) * P],
                                        wh[:, o:o + 512], wl[:, o:o + 512], f == 0, f == 3)
                    ins.then_inc(chunk_used, 1)

            x_transpose(1, None)
            for i in range(4):
                gate_up(1, C_MOE, i, None, None)
            x_transpose(2, 1)
            for i in range(4):
                gate_up(2, C_MOE + 4, i, None, 1)
                if i == 1:
                    a_transpose(1, None)
            x_transpose(3, 2)
            down(1, C_MOE + 8, None, None)
            with pe.Fori(0, NE - 2) as j:
                for i in range(4):
                    gate_up(j + 3, C_MOE + 10, i, j, j + 2)
                    if i == 1:
                        a_transpose(j + 2, j + 1)
                x_transpose(j + 4, j + 3)
                down(j + 2, C_MOE + 14, j, j + 1)
            a_transpose(NE, NE - 1)
            down(NE, C_OVER - 2, None, NE - 1)
            pe.wait_ge(route_ready, 1)
            n_over = pe.value_load(tab[0:1, 0:1], min_val=0, max_val=OVER)
            with pe.Fori(0, OVER) as j:
                with pe.If(n_over > j):
                    for i in range(4):
                        gate_up(j + NE + 1, C_OVER, i, j, j + NE)
                    x_transpose(j + NE + 2, j + NE + 1)
                    a_transpose(j + NE + 1, j + NE)
                    down(j + NE + 1, C_OVER + 4, j, j + NE)
                pe.nop()

        @block.vector
        def _(dve):
            n_link = [0]

            def link(ins):
                n_link[0] += 1
                ins.then_inc(dve_c, 1)
                dve.wait_ge(dve_c, n_link[0])

            def rsqrt(cols, n):
                dve.wait_ge(ss_ready, n)
                link(dve.tensor_scalar(ms[:, cols], ss[:, cols], 1.0 / D, EPS, ALU.mult, ALU.add))
                dve.wait_ge(std_ready, n)
                link(dve.reciprocal(rstd[:, cols], std[:, cols]))
                link(dve.tensor_tensor(ms[:, cols], ms[:, cols], rstd[:, cols], ALU.mult))
                link(dve.tensor_tensor(ms[:, cols], ms[:, cols], rstd[:, cols], ALU.mult))
                link(dve.tensor_scalar(ms[:, cols], ms[:, cols], -0.5, 1.5, ALU.mult, ALU.add))
                link(dve.tensor_tensor(rstd[:, cols], rstd[:, cols], ms[:, cols], ALU.mult))

            rsqrt(slice(0, MB), MB)
            for b in range(MB):
                dve.tensor_scalar(memn[:, b, :], memn[:, b, :], rstd[:, b:b + 1], None, ALU.mult).then_inc(xn_ready, 1)
            split_lo(dve, K(0))
            dve.wait_ge(gains_ps, 1)
            dve.tensor_copy(gains[:, :], bank(7)[:, 0:2 * KD + 2]).then_inc(gains_ready, 1)
            rsqrt(slice(MB, MB + TB), MB + TB)
            for t in range(TB):
                dve.tensor_scalar(xn[:, t, :], xn[:, t, :], rstd[:, MB + t:MB + t + 1], None, ALU.mult).then_inc(xn_ready, 1)
            split_lo(dve, K(1))
            dve.wait_ge(gains_ready, 1)
            for b in range(4):
                dve.wait_ge(memT_h, 2 * b + 2)
                for k in (2 * b, 2 * b + 1):
                    dve.scalar_tensor_tensor(memT_lo[:, k, :], bank(b)[:, (k % 2) * MEM:(k % 2 + 1) * MEM],
                                             gains[:, KD + k:KD + k + 1], memT_hi[:, k, :].bitcast(F32),
                                             ALU.mult, ALU.subtract).then_inc(memT_l, 1)
            for k in range(KD):
                dve.wait_ge(hT_h, k + 1)
                dve.scalar_tensor_tensor(hT_lo[:, k, :], bank(4 + k % 4), gains[:, k:k + 1],
                                         hT_hi[:, k, :].bitcast(F32), ALU.mult, ALU.subtract).then_inc(hT_l, 1)

            def less(dst, src, hi):
                return dve.tensor_tensor(dst, src, hi.bitcast(F32), ALU.subtract)

            def flat(ap):
                return ap.rearrange("p a b -> p (a b)")

            split_lo(dve, K(C_KM + 2))
            dve.wait_ge(proj_h, 1)
            less(flat(km_lo[:, :, :]), bank(0), flat(km_hi[:, :, :])).then_inc(proj_l, 1)
            split_lo(dve, K(C_VM + 2))
            dve.wait_ge(proj_h, 2)
            less(flat(vm_lo[:, :, :]), bank(1), flat(vm_hi[:, :, :])).then_inc(proj_l, 1)
            split_lo(dve, K(C_QX + 2))
            dve.wait_ge(proj_h, 3)
            less(flat(qx_lo[:, :, :]), bank(2, 2), flat(qx_hi[:, :, :])).then_inc(proj_l, 1)
            split_lo(dve, K(C_U + 2))
            dve.memset(pool_u[:, :, 0:U0], 0.0)
            dve.memset(pool_a[:, :, 0:U0], 0.0)
            link(dve.memset(pool_b[:, :, 0:U0], 0.0))
            after(dve, K(C_U))
            dve.tensor_copy(pool_u[:, :, U0:], bank(4, 2).rearrange("p (c t) -> p c t", c=2)).then_inc(pool_d, 1)
            dve.wait_ge(pool_d, 1)

            def window(dst, src, rows, c, shift):
                link(dve.tensor_tensor(dst[rows, c, U0:], src[rows, c, U0:], src[rows, c, U0 - shift:U0 + S - shift], ALU.add))

            lo_r, hi_r, all_r = slice(0, DH), slice(DH, P), slice(0, P)
            sums = ((0, lo_r, 2), (0, hi_r, 4), (1, lo_r, 8), (1, hi_r, 16))
            window(pool_a, pool_u, all_r, 0, 1)
            window(pool_b, pool_a, hi_r, 0, 2)
            link(dve.tensor_copy(pool_a[hi_r, 0, U0:], pool_b[hi_r, 0, U0:]))
            window(pool_a, pool_u, all_r, 1, 1)
            window(pool_b, pool_a, all_r, 1, 2)
            window(pool_a, pool_b, all_r, 1, 4)
            window(pool_b, pool_a, hi_r, 1, 8)
            link(dve.tensor_copy(pool_a[hi_r, 1, U0:], pool_b[hi_r, 1, U0:]))
            dve.wait_ge(consts_ready, 1)
            for c, r, w in sums:
                link(dve.tensor_scalar(inv_n[r, c, :], pos[r, :], float(w), None, ALU.min))
            link(dve.reciprocal(inv_n[:, :, :], inv_n[:, :, :]))
            for c, r, w in sums:
                link(dve.tensor_tensor(pool_a[r, c, U0:U0 + 16], pool_a[r, c, U0:U0 + 16], inv_n[r, c, :], ALU.mult))
                link(dve.tensor_scalar(pool_a[r, c, U0 + 16:], pool_a[r, c, U0 + 16:], 1.0 / w, None, ALU.mult))
            dve.tensor_tensor(pool_a[:, :, U0:], pool_a[:, :, U0:], pool_u[:, :, U0:], ALU.subtract).then_inc(pool_d, 1)
            split_lo(dve, K(C_V + 2))
            dve.wait_ge(proj_h, 4)
            less(flat(v_lo[:, :, :]), bank(0, 4), flat(v_hi[:, :, :])).then_inc(proj_l, 1)
            split_lo(dve, K(C_V + 3))

            def qk_lo(n, b):
                dve.wait_ge(qk_h, n + 1)
                hi, lo = (k_hi, k_lo) if n % 2 else (q_hi, q_lo)
                dve.scalar_tensor_tensor(lo[:, n // 2 % 2, :], bank(b), 1.0 if n % 2 else SCALE,
                                         hi[:, n // 2 % 2, :].bitcast(F32), ALU.mult, ALU.subtract).then_inc(qk_l, 1)

            def cross_max(r):
                dve.wait_ge(xs_ps, r + 1)
                link(dve.tensor_reduce(nmx[:, r, :], bank(4, 4).rearrange("p (i m) -> p i m", m=MEM), AX_X, ALU.max))
                dve.tensor_scalar(nmx[:, r, :], nmx[:, r, :], -SCALE, None, ALU.mult).then_inc(xs_max, 1)

            def cross_norm(r):
                dve.wait_ge(xs_exp, r + 1)
                link(dve.reciprocal(rden[:, r, :], den[:, r, :]))
                for i in range(8):
                    ins = dve.tensor_scalar(probs[:, i, :], probs[:, i, :], rden[:, r, i:i + 1], None, ALU.mult)
                ins.then_inc(xs_norm, 1)

            def cross_t(r):
                dve.wait_ge(xt_h, r + 1)
                less(flat(pT_lo[:, :, :]), bank(4, 4), flat(pT_hi[:, :, :])).then_inc(xt_l, 1)

            def cross_o(r):
                dve.wait_ge(xo_h, r + 1)
                for h in range(2):
                    rows = slice(DH * h, DH * h + DH)
                    ins = less(xaT_lo[rows, r, :], bank(h)[rows, :], xaT_hi[rows, r, :])
                ins.then_inc(xo_l, 1)

            cross_max(0)
            dve.wait_ge(pool_h, 2)
            for c in range(2):
                dve.scalar_tensor_tensor(plT_lo[:, c, :], bank(c), gains[:, 2 * KD + c:2 * KD + c + 1],
                                         plT_hi[:, c, :].bitcast(F32), ALU.mult, ALU.subtract).then_inc(pool_l, 1)
            cross_norm(0)
            split_lo(dve, K(C_PAIR + 2))
            qk_lo(0, 2)
            qk_lo(1, 3)
            cross_t(0)
            split_lo(dve, K(C_PAIR + 3))
            qk_lo(2, 2)
            qk_lo(3, 3)
            cross_o(0)
            cross_max(1)
            cross_norm(1)
            cross_t(1)
            cross_o(1)

            for n in range(HEADS + 2):
                z = bank(3 * (n % 2), 3)[:, 0:ZW]
                if n < HEADS:
                    dve.wait_ge(z_ps, n + 1)
                    if n >= 1:
                        dve.wait_ge(soft_l, n)
                    dve.tensor_scalar(soft[:, :].bitcast(U32), z.bitcast(U32), 0x7FFFFFFF, None, ALU.bitwise_and).then_inc(z_abs, 1)
                    dve.wait_ge(z_ln, n + 1)
                    dve.scalar_tensor_tensor(soft[:, :], z, 0.0, soft[:, :], ALU.max, ALU.add).then_inc(z_soft, 1)
                    dve.wait_ge(soft_h, n + 1)
                    dve.tensor_tensor(soft_lo[:, :], soft[:, :], soft_hi[:, :].bitcast(F32), ALU.subtract).then_inc(soft_l, 1)
                if 1 <= n <= HEADS:
                    dve.wait_ge(a_exp, n)
                    if n >= 2:
                        dve.wait_ge(av_ps, n - 1)
                    dve.tensor_copy(attn_hi[:, :], attn[:, :]).then_inc(a_h, 1)
                    dve.wait_ge(a_h, n)
                    dve.tensor_tensor(attn_lo[:, :], attn[:, :], attn_hi[:, :].bitcast(F32), ALU.subtract).then_inc(a_l, 1)
                if n in (2, 4):
                    split_lo(dve, K(C_MERGE + (n - 2) // 2))
                if n >= 2:
                    m = n - 2
                    rows = slice(DH * (m % 2), DH * (m % 2) + DH)
                    dve.wait_ge(av_h, m + 1)
                    less(sbT_lo[rows, m // 2, :], bank(7)[rows, :], sbT_hi[rows, m // 2, :]).then_inc(av_l, 1)
                if 2 <= n < 6:
                    qk_lo(n + 2, 6)

            dve.wait_ge(av_ps, HEADS)
            dve.sem_inc(b_used, 3)
            two = lambda b: bank(b, 2).rearrange("p (c t) -> p c t", c=2)
            with dve.Fori(0, KD // 2) as dp:
                for i in range(PER_DP):
                    split_lo(dve, K(C_MERGE + i + 2, dp, PER_DP), width_of(C_MERGE + (i + 2) % PER_DP))
                    if i >= 3:
                        j = i - 3
                        after(dve, K(C_MERGE + i, dp, PER_DP))
                        if j == 2:
                            dve.wait_ge(b_add, dp + 1)
                        dst = merged if j == 0 else branch
                        dve.tensor_tensor(dst[:, :, :], two(2 * j), sig[:, j, :, :], ALU.mult).then_inc(b_used, 1)
                        if j > 0:
                            dve.wait_ge(b_used, dp * 3 + 3 + j + 1)
                        if j > 0:
                            dve.tensor_tensor(merged[:, :, :], merged[:, :, :], branch[:, :, :], ALU.add) \
                               .then_inc(b_add if j == 1 else mg_ready, 1)
                dve.wait_ge(mg_h, dp + 1)
                dve.tensor_tensor(mgT_lo[:, bass.ds(dp * 2, 2), :], merged[:, :, :],
                                  mgT_hi[:, bass.ds(dp * 2, 2), :].bitcast(F32), ALU.subtract).then_inc(mg_l, 1)
            dve.wait_ge(xres_in, 16)
            for half in range(2):
                split_lo(dve, K(C_OUT + 2 * half + 2))
                split_lo(dve, K(C_OUT + 2 * half + 3))
                after(dve, K(C_OUT + 2 * half + 1))
                cols = slice(half * 512, half * 512 + 512)
                dve.tensor_tensor(x2[:, :, cols], bank(4 * half, 4).rearrange("p (t n) -> p t n", t=TB),
                                  x2[:, :, cols], ALU.add).then_inc(x2_ready, 1)
            split_lo(dve, K(C_MOE + 2))

            dve.wait_ge(gffn_in, 16)
            rsqrt(slice(8, 12), MB + 2 * TB)
            for t in range(TB):
                dve.scalar_tensor_tensor(h2[:, t, :], x2[:, t, :], rstd[:, 8 + t:9 + t], gffn_bc[:, :],
                                         ALU.mult, ALU.mult).then_inc(h2_ready, 1)
            for k in range(1, KD, 2):
                dve.wait_ge(h2T_ps, k + 1)
                dve.tensor_copy(h2T[:, k, :], bank(k % 4)).then_inc(h2T_v, 1)
            dve.wait_ge(lg_ps, 1)
            dve.wait_ge(small_in, 16 * 8)
            lgw = NG + NE
            for t in range(TB):
                ins = dve.tensor_tensor(lgs[:, t, :], bank(4)[:, t * lgw:(t + 1) * lgw], bias_bc[:, :], ALU.add)
                link(ins)
            gl, el = lgs[:, :, 0:NG], lgs[:, :, NG:lgw]

            def row(v, n):
                return v[:, :].unsqueeze(2).broadcast_to([P, TB, n])

            def each(v, n):
                return v[:, 0:n].unsqueeze(1).broadcast_to([P, TB, n])

            def first_max(dst, vals, mx, lowest, tmp, n):
                link(dve.tensor_reduce(mx[:, :], vals, AX_X, ALU.max))
                link(dve.tensor_tensor(tmp, vals, row(mx, n), ALU.is_equal))
                link(dve.tensor_tensor(tmp, tmp, each(jm, n), ALU.mult))
                link(dve.tensor_reduce(lowest[:, :], tmp, AX_X, ALU.min))
                link(dve.tensor_tensor(dst, each(jm, n), row(lowest, n), ALU.is_equal))

            tmp, gsel, elm, m1, m2 = (r[:, :, :] for r in rt[0:5])
            gmax, lowest, v1, v2 = sm[0:4]
            first_max(gsel[:, :, 0:NG], gl, gmax, lowest, tmp[:, :, 0:NG], NG)
            link(dve.tensor_scalar(gsel[:, :, 0:NG], gsel[:, :, 0:NG], 1.0, BIG, ALU.subtract, ALU.mult))
            for g in range(NG):
                cols = slice(g * EPG, (g + 1) * EPG)
                ins = dve.tensor_tensor(elm[:, :, cols], el[:, :, cols],
                                        gsel[:, :, g:g + 1].broadcast_to([P, TB, EPG]), ALU.add)
            link(ins)
            first_max(m1, elm, v1, lowest, tmp, NE)
            link(dve.scalar_tensor_tensor(elm, m1, -BIG, elm, ALU.mult, ALU.add))
            first_max(m2, elm, v2, lowest, tmp, NE)
            dve.tensor_tensor(onehot_b[:, :, :], m1, m2, ALU.add).then_inc(onehot_ready, 1)
            link(dve.tensor_tensor(ex[:, :, 0:NG], gl, row(gmax, NG), ALU.subtract))
            dve.tensor_tensor(ex[:, :, 4:5], v2[:, :].unsqueeze(2), v1[:, :].unsqueeze(2), ALU.subtract).then_inc(r_max, 1)
            rank, q, slot, t0 = (r[:, :, :] for r in rt[5:9])
            n_tok, extra, base1, obase = (r[:, 0, :] for r in rt[9:13])
            dve.wait_ge(rank_ps, 1)
            link(dve.tensor_copy(rank, bank(5)[:, 0:TB * NE].rearrange("p (t e) -> p t e", t=TB)))
            link(dve.tensor_copy(n_tok, bank(5)[:, TB * NE:(TB + 1) * NE]))
            link(dve.tensor_scalar(extra, n_tok, float(P), None, ALU.is_gt))
            for m in range(2, TB):
                link(dve.scalar_tensor_tensor(extra, n_tok, float(m * P), extra, ALU.is_gt, ALU.add))
            link(dve.memset(pre[0][:, :], 0.0))
            link(dve.memset(pre[1][:, :], 0.0))
            link(dve.tensor_copy(pre[0][:, 8:8 + NE], extra))
            for i, sh in enumerate((1, 2, 4, 8)):
                a, b = pre[i % 2], pre[(i + 1) % 2]
                link(dve.tensor_tensor(b[:, 8:8 + NE], a[:, 8:8 + NE], a[:, 8 - sh:8 + NE - sh], ALU.add))
            incl = pre[0][:, 8:8 + NE]
            link(dve.tensor_tensor(obase, incl, extra, ALU.subtract))
            link(dve.tensor_scalar(base1, obase, float(P), float((NE - 1) * P), ALU.mult, ALU.add))
            link(dve.tensor_tensor(base1, base1, e128[:, :], ALU.subtract))
            link(dve.tensor_scalar(q, rank, float(P), None, ALU.is_ge))
            bc = lambda v: v.unsqueeze(1).broadcast_to([P, TB, NE])
            link(dve.tensor_tensor(q, q, bc(base1), ALU.mult))
            link(dve.tensor_tensor(slot, rank, bc(e128[:, :]), ALU.add))
            link(dve.tensor_tensor(slot, slot, q, ALU.add))
            for r, mm in ((0, m1), (1, m2)):
                link(dve.tensor_tensor(t0, mm, slot, ALU.mult))
                link(dve.tensor_reduce(sm[4 + r][:, :], t0, AX_X, ALU.add))
                link(dve.tensor_copy(slot_u[:, r, :], sm[4 + r][:, :]))
            link(dve.tensor_tensor(cmp_t[:, :, :], incl.unsqueeze(1).broadcast_to([P, OVER, NE]),
                                   pos[:, 0:OVER].unsqueeze(2).broadcast_to([P, OVER, NE]), ALU.is_lt))
            link(dve.tensor_reduce(rt[13][:, 0, 1:1 + OVER], cmp_t[:, :, :], AX_X, ALU.add))
            link(dve.tensor_scalar(rt[13][:, 0, 1:1 + OVER], rt[13][:, 0, 1:1 + OVER], float(NE - 1), None, ALU.min))
            link(dve.tensor_copy(rt[13][:, 0, 0:1], incl[:, NE - 1:NE]))
            dve.tensor_copy(tab[:, :], rt[13][:, 0, 0:8]).then_inc(route_ready, 1)
            dve.wait_ge(r_exp, 1)
            link(dve.tensor_reduce(sm[0][:, :], ex[:, :, 0:NG], AX_X, ALU.add))
            e2 = ex[:, :, 4:5].rearrange("p t o -> p (t o)")
            link(dve.tensor_scalar(sm[1][:, :], e2, 1.0, None, ALU.add))
            link(dve.tensor_tensor(sm[0][:, :], sm[0][:, :], sm[1][:, :], ALU.mult))
            link(dve.reciprocal(wts[:, 0, :], sm[0][:, :]))
            link(dve.tensor_tensor(wts[:, 1, :], wts[:, 0, :], e2, ALU.mult))

            def xe_lo(n):
                dve.wait_ge(xe_h, n)
                dve.tensor_tensor(xT_lo[:, :], bank(2, 2), xT_hi[:, :].bitcast(F32), ALU.subtract).then_inc(xe_l, 1)

            def gated(n):
                dve.wait_ge(silu_ready, n)
                dve.tensor_tensor(act_e[:, :], bank(1), silu_g[:, :], ALU.mult).then_inc(act_ready, 1)

            def aT_l(n):
                dve.wait_ge(at_h, n)
                dve.tensor_tensor(aT_lo[:, :], bank(4), aT_hi[:, :].bitcast(F32), ALU.subtract).then_inc(at_l, 1)

            def y_half(c, stored):
                after(dve, c)
                if stored is not None:
                    dve.wait_ge(y_out, stored)
                dve.tensor_copy(ye[:, 512:1024], bank(6)).then_inc(y_v, 1)

            xe_lo(1)
            for i in range(1, 4):
                split_lo(dve, K(C_MOE + i + 2))
            gated(1)
            xe_lo(2)
            for i in range(PER_E):
                split_lo(dve, K(C_MOE + 4 + i + 2))
                if i == 1:
                    aT_l(1)
                if i == 3:
                    gated(2)
                    xe_lo(3)
            y_half(K(C_MOE + 9), None)
            with dve.Fori(0, NE - 2) as j:
                for i in range(PER_E):
                    split_lo(dve, K(C_MOE + 10 + i + 2, j, PER_E))
                    if i == 1:
                        aT_l(j + 2)
                    if i == 3:
                        gated(j + 3)
                        xe_lo(j + 4)
                y_half(K(C_MOE + 15, j, PER_E), (j + 1) * 16)
            aT_l(NE)
            y_half(K(C_OVER - 1), 16 * (NE - 1))
            n_over = dve.value_load(tab[0:1, 0:1], min_val=0, max_val=OVER)
            with dve.Fori(0, OVER) as j:
                with dve.If(n_over > j):
                    for i in range(PER_E):
                        split_lo(dve, K(C_OVER + i, j, PER_E))
                    gated(j + NE + 1)
                    xe_lo(j + NE + 2)
                    aT_l(j + NE + 1)
                    y_half(K(C_OVER + 5, j, PER_E), (j + NE) * 16)
                dve.nop()

            dve.wait_ge(gfin_in, 16)
            for t in range(TB + 1):
                if t < TB:
                    dve.wait_ge(yg_in[t % 2], 32 * (t // 2 + 1))
                    link(dve.scalar_tensor_tensor(x2[:, t, :], y1[:, t % 2, :], wts[:, 0, t:t + 1], x2[:, t, :],
                                                  ALU.mult, ALU.add))
                    dve.scalar_tensor_tensor(x2[:, t, :], y2[:, t % 2, :], wts[:, 1, t:t + 1], x2[:, t, :],
                                             ALU.mult, ALU.add).then_inc(comb_ready, 1)
                if t >= 1:
                    u = t - 1
                    rsqrt(slice(12 + u, 13 + u), MB + 2 * TB + u + 1)
                    dve.scalar_tensor_tensor(x2[:, u, :], x2[:, u, :], rstd[:, 12 + u:13 + u], gfin_bc[:, :],
                                             ALU.mult, ALU.mult).then_inc(res_ready, 1)


_INS = ["x", "mem", "norm_mix", "norm_mem", "w_in", "w_pool", "pool_scale", "w_kv_mem", "w_up_sb", "w_up_pool",
        "w_up_x", "w_out", "norm_ffn", "w_group", "b_group", "w_router", "b_router", "w_gate", "w_up", "w_down",
        "norm_final"]


def kernel(**inputs):
    import numpy as np
    import concourse.bacc as bacc
    from concourse.bass_utils import run_bass_kernel_spmd

    nc = bacc.Bacc("TRN2", target_bir_lowering=False, num_devices=1)
    arrays, args = {}, []
    for name in _INS:
        a = np.ascontiguousarray(inputs[name])
        arrays[f"in_{name}"] = a
        args.append(nc.dram_tensor(f"in_{name}", a.shape, mybir.dt.from_np(a.dtype), kind="ExternalInput").ap())
    args.append(nc.dram_tensor("out_0", (1, S, D), F32, kind="ExternalOutput").ap())
    build_trunk(nc, *args)
    r = run_bass_kernel_spmd(nc, [arrays], core_ids=[0])
    return r.results[0]["out_0"]
```

```python
from contextlib import ExitStack

import concourse.bass as bass
from concourse import mybir

F32 = mybir.dt.float32
F32R = mybir.dt.float32r
BF16 = mybir.dt.bfloat16
I32 = mybir.dt.int32
U32 = mybir.dt.uint32
ALU = mybir.AluOpType
ACT = mybir.ActivationFunctionType
AX_X = mybir.AxisListType.X

P = 128
EPS = 1e-6
BIG = 1e30
NEG = -float(2 ** 100)

D = 1024
S = 512
MEM = 256
DH = 64
HEADS = 8
XHEADS = 4
SBW = 512
PW = 256
XW = 256
NG, EPG, NE, FF = 4, 4, 16, 512
KD = D // P
TB = S // P
MB = MEM // P
COL_K, COL_V, COL_U, COL_QX, COL_G = 512, 1024, 1536, 1792, 2048
SCALE = DH ** -0.5

OVER = (2 * S - 1) // P
TILES = NE + OVER
SLOT_TILES = TILES + 1
NO_ROW = 4 * S

CW = 2048
SPLIT = 3
RAW = 3
RAW_MOE = 12
RAW_OVER = 6
IN_FLIGHT = 4
FULL = 64
C_KM, C_VM, C_QX, C_U, C_V, C_PAIR = 0, 1, 2, 3, 4, 6
C_MERGE = C_PAIR + HEADS // 2
PER_DP = 6
C_OUT = C_MERGE + PER_DP * (KD // 2)
C_MOE = C_OUT + 4
PER_E = 6
C_OVER = C_MOE + PER_E * NE
assert PER_DP % SPLIT == 0 and PER_E % SPLIT == 0 and RAW_MOE == 2 * PER_E and NE % 2 == 0

ZOFF = {0: 0, 1: 512, 3: 896, 2: 1024}
ZN = {sb: S - P * sb for sb in range(TB)}
ZW = 1280


def stage_map(base):
    at = {}
    o = base
    for name, size in (("const", 9216), ("ring_hi", 4 * CW * SPLIT), ("ring_lo", 4 * CW * SPLIT),
                       ("raw", 4 * CW * RAW), ("m", 98304), ("t", 30720)):
        at[name] = o
        o += size
    at["end"] = o
    return at


def build_trunk(nc, x, mem, norm_mix, norm_mem, w_in, w_pool, pool_scale, w_kv_mem, w_up_sb,
                w_up_pool, w_up_x, w_out, norm_ffn, w_group, b_group, w_router, b_router,
                w_gate, w_up, w_down, norm_final, out):
    base = (nc.sbuf_base + 63) // 64 * 64
    at = stage_map(base)
    assert at["end"] <= nc.sbuf_usable_end, at

    cursor = {}

    def sb(name, shape, dt, region, offset=None):
        size = 1
        for n in shape[1:]:
            size *= n
        size *= 2 if dt == BF16 else 4
        if offset is None:
            offset = cursor.get(region, 0)
            cursor[region] = offset + (size + 31) // 32 * 32
        return nc.alloc_sbuf_tensor_at(name, shape, dt, offset=at[region] + offset)

    KB = 1024
    ident = sb("ident", [P, P], F32, "const")
    identb = sb("identb", [P, P], BF16, "const")
    negmask = sb("negmask", [P, P], BF16, "const")
    tri_f = sb("tri_f", [P, P], F32, "const")
    negtri = sb("negtri", [P, P], F32R, "const")
    negones = sb("negones", [P, P], F32R, "const")
    rank_tri = sb("rank_tri", [P, P], BF16, "const")
    ones_b = sb("ones_b", [P, P], BF16, "const")
    gain_rows = sb("gain_rows", [2 * KD + 2, P], F32, "const")
    gains = sb("gains", [P, 2 * KD + 2], F32, "const")
    wr = sb("wr", [P, KD, NG + NE], F32, "const")
    bias_bc = sb("bias_bc", [P, NG + NE], F32, "const")
    pos = sb("pos", [P, 16], F32, "const")
    inv_n = sb("inv_n", [P, 2, 16], F32, "const")
    wp = sb("wp", [P, 2, P], F32, "const")
    ss = sb("ss", [P, 16], F32, "const")
    rstd = sb("rstd", [P, 16], F32, "const")
    std = sb("std", [P, 16], F32, "const")
    ms = sb("ms", [P, 16], F32, "const")
    eps_c = sb("eps_c", [P, 1], F32, "const")
    nmx = sb("nmx", [P, 2, 8], F32, "const")
    den = sb("den", [P, 2, 8], F32, "const")
    rden = sb("rden", [P, 2, 8], F32, "const")
    jm = sb("jm", [P, NE], F32, "const")
    e128 = sb("e128", [P, NE], F32, "const")
    wts = sb("wts", [P, 2, TB], F32, "const")
    slot_f = sb("slot_f", [P, 2 * TB], F32, "const")
    slot_i = sb("slot_i", [P, 2 * TB], I32, "const")
    part_i = sb("part_i", [P, 2 * TB], I32, "const")
    tile_i = sb("tile_i", [P, 2 * TB], I32, "const")
    tab = sb("tab", [P, 8], I32, "const")
    before = sb("before", [P, NE, NE], F32, "const")
    base_c = sb("base_c", [P, NE], F32, "const")
    slot_no = sb("slot_no", [P, P], I32, "const")
    tile_no = sb("tile_no", [P, SLOT_TILES], I32, "const")
    id_block = sb("id_block", [P, 2 * TB], F32, "const")
    id_row = sb("id_row", [P, 2 * TB], F32, "const")
    y_row = sb("y_row", [P, SLOT_TILES], I32, "const")
    x_row = sb("x_row", [P, SLOT_TILES], I32, "const")
    x_col = [sb(f"x_col{b}", [P, 1], I32, "const") for b in range(2)]
    y_col = [sb(f"y_col{b}", [P, 1], I32, "const") for b in range(2)]
    lgs = sb("lgs", [P, TB, NG + NE], F32, "const")
    ex = sb("ex", [P, TB, 8], F32, "const")
    sm = [sb(f"sm{i}", [P, TB], F32, "const") for i in range(8)]
    assert cursor["const"] <= at["ring_hi"] - at["const"], cursor

    ring_hi = sb("ring_hi", [P, SPLIT, CW], F32R, "ring_hi", 0)
    ring_lo = sb("ring_lo", [P, SPLIT, CW], F32R, "ring_lo", 0)
    raw_a = sb("raw_a", [P, RAW, CW], F32, "raw", 0)

    hT_hi = sb("hT_hi", [P, KD, S], F32R, "m", 0)
    hT_lo = sb("hT_lo", [P, KD, S], F32R, "m", 16 * KB)
    v_hi = sb("v_hi", [P, TB, SBW], F32R, "m", 32 * KB)
    v_lo = sb("v_lo", [P, TB, SBW], F32R, "m", 40 * KB)
    q_hi = sb("q_hi", [P, 2, S], F32R, "m", 48 * KB)
    q_lo = sb("q_lo", [P, 2, S], F32R, "m", 52 * KB)
    k_hi = sb("k_hi", [P, 2, S], F32R, "m", 56 * KB)
    k_lo = sb("k_lo", [P, 2, S], F32R, "m", 60 * KB)
    sbT_hi = sb("sbT_hi", [P, 4, S], F32R, "m", 64 * KB)
    sbT_lo = sb("sbT_lo", [P, 4, S], F32R, "m", 72 * KB)
    plT_hi = sb("plT_hi", [P, 2, S], F32R, "m", 80 * KB)
    plT_lo = sb("plT_lo", [P, 2, S], F32R, "m", 84 * KB)
    xaT_hi = sb("xaT_hi", [P, 2, S], F32R, "m", 88 * KB)
    xaT_lo = sb("xaT_lo", [P, 2, S], F32R, "m", 92 * KB)
    memT_hi = sb("memT_hi", [P, KD, MEM], F32R, "m", 64 * KB)
    memT_lo = sb("memT_lo", [P, KD, MEM], F32R, "m", 72 * KB)
    pT_hi = sb("pT_hi", [P, 4, S], F32R, "m", 64 * KB)
    pT_lo = sb("pT_lo", [P, 4, S], F32R, "m", 72 * KB)
    mgT_hi = sb("mgT_hi", [P, KD, S], F32R, "m", 32 * KB)
    mgT_lo = sb("mgT_lo", [P, KD, S], F32R, "m", 48 * KB)
    xn = sb("xn", [P, TB, D], F32, "t", 0)
    memn = sb("memn", [P, MB, D], F32, "t", 16 * KB)
    junk = sb("junk", [P, D], F32, "t", 24 * KB)
    qx_hi = sb("qx_hi", [P, 2, S], F32R, "t", 0)
    qx_lo = sb("qx_lo", [P, 2, S], F32R, "t", 4 * KB)
    km_hi = sb("km_hi", [P, 2, MEM], F32R, "t", 8 * KB)
    km_lo = sb("km_lo", [P, 2, MEM], F32R, "t", 10 * KB)
    vm_hi = sb("vm_hi", [P, MB, XW], F32R, "t", 12 * KB)
    vm_lo = sb("vm_lo", [P, MB, XW], F32R, "t", 14 * KB)
    U0 = 16
    pool_u = sb("pool_u", [P, 2, U0 + S], F32, "t", 16 * KB)
    pool_b = sb("pool_b", [P, 2, U0 + S], F32, "t", 16 * KB + 4224)
    pool_a = sb("pool_a", [P, 2, U0 + S], F32, "t", 16 * KB + 8448)
    probs = sb("probs", [P, 8, MEM], F32, "t", 16 * KB)
    log_in = sb("log_in", [P, ZW], F32, "t", 0)
    soft = sb("soft", [P, ZW], F32, "t", 5 * KB)
    soft_lo = sb("soft_lo", [P, ZW], F32R, "t", 5 * KB)
    soft_hi = sb("soft_hi", [P, ZW], F32R, "t", 10 * KB)
    attn_hi = sb("attn_hi", [P, ZW], F32R, "t", 15 * KB)
    attn = [sb(f"attn{b}", [P, ZW], F32, "t", (20 + 5 * b) * KB) for b in range(2)]
    attn_lo = [sb(f"attn_lo{b}", [P, ZW], F32R, "t", (20 + 5 * b) * KB) for b in range(2)]
    sig = sb("sig", [P, 3, 2, S], F32, "t", 0)
    merged = sb("merged", [P, 2, S], F32, "t", 12 * KB)
    branch = sb("branch", [P, 2, S], F32, "t", 16 * KB)
    gffn_bc = sb("gffn_bc", [P, D], F32, "t", 24 * KB)
    x2 = sb("x2", [P, TB, D], F32, "m", 0)
    h2 = sb("h2", [P, TB, D], F32, "m", 16 * KB)
    h2T = sb("h2T", [P, TB, KD, P], F32, "t", 0)
    rt = [sb(f"rt{i}", [P, TB, NE], F32, "t", 16 * KB + 256 * i) for i in range(16)]
    onehot_b = sb("onehot_b", [P, TB, NE], BF16, "t", 20 * KB)
    cmp_t = sb("cmp_t", [P, OVER, NE], F32, "t", 21 * KB)
    picked = sb("picked", [P, 2, TB, NE], F32, "t", 22 * KB)
    picked_slot = sb("picked_slot", [P, 2, TB, NE], F32, "t", 22 * KB + 512)
    at_part = sb("at_part", [P, 2 * TB, P], BF16, "m", 48 * KB)
    at_tile = sb("at_tile", [P, 2 * TB, SLOT_TILES], F32, "m", 50 * KB)
    at_block = sb("at_block", [P, 2 * TB, SLOT_TILES], BF16, "m", 51 * KB)
    at_row = sb("at_row", [P, 2 * TB, SLOT_TILES], BF16, "m", 52 * KB)
    ex_before = sb("ex_before", [P, NE, NE], F32, "m", 53 * KB)
    raw_moe = [raw_a[:, s, :] for s in range(RAW)] + [
        sb(f"raw{RAW + s}", [P, CW], F32, region, o * KB)[:, :] for s, (region, o) in enumerate((
            ("m", 88), ("m", 64), ("m", 72), ("m", 80),
            ("m", 16), ("m", 24),
            ("t", 0), ("t", 8),
            ("t", 16)))]
    assert len(raw_moe) == RAW_MOE
    xe = [sb("xe0", [P, D], F32, "m", 56 * KB), sb("xe1", [P, D], F32, "t", 24 * KB)]
    xT_hi = sb("xT_hi", [P, D], F32R, "m", 32 * KB)
    xT_lo = sb("xT_lo", [P, D], F32R, "m", 36 * KB)
    silu_g = sb("silu_g", [P, FF], F32, "m", 40 * KB)
    act_e = sb("act_e", [P, FF], F32, "m", 42 * KB)
    aT_hi = sb("aT_hi", [P, FF], F32R, "m", 44 * KB)
    aT_lo = sb("aT_lo", [P, FF], F32R, "m", 46 * KB)
    ye = [sb("ye0", [P, D], F32, "m", 48 * KB), sb("ye1", [P, D], F32, "m", 52 * KB)]
    y_in = sb("y_in", [P, TB, 2, D], F32, "m", 16 * KB)
    junk2 = sb("junk2", [P, D], F32, "t", 20 * KB)
    gfin_bc = sb("gfin_bc", [P, D], F32, "m", 60 * KB)
    junk3 = sb("junk3", [P, D], F32, "m", 52 * KB)

    ps = nc.alloc_psum_tensor("ps", [P, 8 * 512], F32)

    def bank(b, n=1):
        return ps[:, 512 * b:512 * (b + n)]

    h2_rows = nc.dram_tensor("h2_rows", [S, D], F32, kind="Internal").ap()
    y_rows = nc.dram_tensor("y_rows", [2 * S, D], F32, kind="Internal").ap()

    ctx = ExitStack()
    with ctx:
        sems = {}

        def sem(name):
            sems[name] = ctx.enter_context(nc.semaphore(name))
            return sems[name]

        consts_ready = sem("consts_ready")
        consts_mem = sem("consts_mem")
        gain_in = sem("gain_in")
        mem_in = sem("mem_in")
        sp_free = sem("sp_free")
        x_in = [sem(f"x_in{t}") for t in range(TB)]
        small_in = sem("small_in")
        raw_full = [sem(f"raw_full{s}") for s in range(RAW_MOE)]
        hi_ready = sem("hi_ready")
        lo_ready = sem("lo_ready")
        chunk_used = sem("chunk_used")
        act_c = sem("act_c")
        dve_c = sem("dve_c")
        consts_r = sem("consts_r")
        ss_ready = sem("ss_ready")
        std_ready = sem("std_ready")
        xn_ready = sem("xn_ready")
        gains_ps = sem("gains_ps")
        gains_ready = sem("gains_ready")
        memT_ps = sem("memT_ps")
        memT_h = sem("memT_h")
        memT_l = sem("memT_l")
        hT_ps = sem("hT_ps")
        hT_h = sem("hT_h")
        hT_l = sem("hT_l")
        proj_h = sem("proj_h")
        proj_l = sem("proj_l")
        pool_d = sem("pool_d")
        pool_ps = sem("pool_ps")
        pool_h = sem("pool_h")
        pool_l = sem("pool_l")
        q_ps = sem("q_ps")
        qk_h = sem("qk_h")
        qk_l = sem("qk_l")
        xs_ps = sem("xs_ps")
        xs_max = sem("xs_max")
        xs_exp = sem("xs_exp")
        xs_norm = sem("xs_norm")
        xt_ps = sem("xt_ps")
        xt_h = sem("xt_h")
        xt_l = sem("xt_l")
        xo_ps = sem("xo_ps")
        xo_h = sem("xo_h")
        xo_l = sem("xo_l")
        z_ps = sem("z_ps")
        z_ln = sem("z_ln")
        z_soft = sem("z_soft")
        soft_h = sem("soft_h")
        soft_l = sem("soft_l")
        tail_ps = sem("tail_ps")
        a_exp = sem("a_exp")
        a_h = sem("a_h")
        a_l = sem("a_l")
        av_ps = sem("av_ps")
        av_h = sem("av_h")
        av_l = sem("av_l")
        g_sig = sem("g_sig")
        b_used = sem("b_used")
        b_add = sem("b_add")
        mg_ready = sem("mg_ready")
        mg_h = sem("mg_h")
        mg_l = sem("mg_l")
        xres_in = sem("xres_in")
        x2_half = sem("x2_half")
        x2_ready = sem("x2_ready")
        o_ps = sem("o_ps")
        gffn_in = sem("gffn_in")
        gfin_in = sem("gfin_in")
        h2_ready = sem("h2_ready")
        h2T_ps = sem("h2T_ps")
        h2T_a = sem("h2T_a")
        h2T_v = sem("h2T_v")
        lg_ps = sem("lg_ps")
        r_max = sem("r_max")
        r_exp = sem("r_exp")
        onehot_ready = sem("onehot_ready")
        rank_ps = sem("rank_ps")
        route_ready = sem("route_ready")
        sel_ready = sem("sel_ready")
        rows_ps = sem("rows_ps")
        rows_ready = sem("rows_ready")
        h2_out = sem("h2_out")
        pool_free = sem("pool_free")
        xe_clear = sem("xe_clear")
        x_col_set = sem("x_col_set")
        y_col_set = sem("y_col_set")
        xe_in = [sem("xe_in0"), sem("xe_in1")]
        xe_ps = sem("xe_ps")
        xe_h = sem("xe_h")
        xe_l = sem("xe_l")
        silu_ready = sem("silu_ready")
        act_ready = sem("act_ready")
        at_ps = sem("at_ps")
        at_h = sem("at_h")
        at_l = sem("at_l")
        y_a = sem("y_a")
        y_v = sem("y_v")
        y_out = [sem("y_out0"), sem("y_out1")]
        ye_free = sem("ye_free")
        y_back = [sem(f"y_back{t}") for t in range(TB)]
        comb_ready = sem("comb_ready")
        res_ready = sem("res_ready")
        out_done = sem("out_done")

        block = ctx.enter_context(nc.Block())

        def raw_slot(c):
            c0 = c[0]
            if c0 < C_MOE:
                return raw_a[:, c0 % RAW, :], raw_full[c0 % RAW]
            s = (c0 - C_MOE) % RAW_MOE if c0 < C_OVER else (c0 - C_OVER) % RAW_OVER
            return raw_moe[s], raw_full[s]

        def raw_count(c):
            c0, i, per = c
            if c0 < C_MOE:
                n, ring = c0 // RAW + 1, RAW
            else:
                m = c0 - C_MOE if c0 < C_OVER else c0 - C_OVER
                ring = RAW_MOE if c0 < C_OVER else RAW_OVER
                s = m % ring
                n = (len(range(s, C_MOE, RAW)) if s < RAW else 0) + m // ring + 1
                if c0 >= C_OVER:
                    n += (C_OVER - C_MOE) // RAW_MOE
            return FULL * n if i is None else FULL * n + i * (FULL * (per // ring))

        def upto(c, less=0):
            c0, i, per = c
            n = c0 + 1 - less
            return n if i is None else n + i * per

        def split_hi(act, c, width=CW):
            buf, full = raw_slot(c)
            act.wait_ge(full, raw_count(c))
            if c[0] >= SPLIT or c[1] is not None:
                act.wait_ge(chunk_used, upto(c, SPLIT))
            act.activation(ring_hi[:, c[0] % SPLIT, 0:width], buf[:, 0:width], ACT.Copy).then_inc(hi_ready, 1)

        def split_lo(dve, c, width=CW):
            buf, _ = raw_slot(c)
            s = c[0] % SPLIT
            dve.wait_ge(hi_ready, upto(c))
            dve.tensor_tensor(ring_lo[:, s, 0:width], buf[:, 0:width],
                              ring_hi[:, s, 0:width].bitcast(F32), ALU.subtract).then_inc(lo_ready, 1)

        def K(c0, i=None, per=0):
            return (c0, i, per)

        def after(eng, c):
            eng.wait_ge(chunk_used, upto(c))

        def width_of(c0):
            if C_MERGE <= c0 < C_OUT:
                return (CW, CW, CW, CW // 2, CW // 4, CW // 4)[(c0 - C_MERGE) % PER_DP]
            return CW

        def three(pe, out_ap, l_hi, l_lo, r_hi, r_lo, start, stop):
            pe.matmul(out_ap, l_hi, r_hi, start=start, stop=False, skip_group_check=True)
            pe.matmul(out_ap, l_hi, r_lo, start=False, stop=False, skip_group_check=True)
            return pe.matmul(out_ap, l_lo, r_hi, start=False, stop=stop, skip_group_check=True)

        @block.sync
        def _(sp):
            sp.dma_start(gain_rows[0:KD, :], norm_mix[0].rearrange("(k p) -> k p", p=P)).then_inc(gain_in, 16)
            sp.dma_start(gain_rows[KD:2 * KD, :], norm_mem[0].rearrange("(k p) -> k p", p=P)).then_inc(gain_in, 16)
            sp.dma_start(gain_rows[2 * KD:2 * KD + 2, :], pool_scale[0].rearrange("(k p) -> k p", p=P)).then_inc(gain_in, 16)
            sp.dma_start(memn[:, :, :], mem[0].rearrange("(b p) d -> p b d", p=P)).then_inc(mem_in, 16)

            def load(c, pieces):
                buf, full = raw_slot(c)
                for (a, b, shape), src in pieces:
                    dst = buf[:, a:b].rearrange("p (k n) -> p k n", k=shape)
                    sp.dma_start(dst, src).then_inc(full, FULL // len(pieces))

            def rows(w, k0, k1, c0, c1):
                return w[k0 * P:k1 * P, c0:c1].rearrange("(k p) n -> p k n", p=P)

            win = w_in[0]
            wkv = w_kv_mem[0]
            load(K(C_KM), [((0, CW, KD), rows(wkv, 0, KD, 0, XW))])
            for t in range(TB):
                sp.dma_start(xn[:, t, :], x[0, t * P:(t + 1) * P, :]).then_inc(x_in[t], 16)
            load(K(C_VM), [((0, CW, KD), rows(wkv, 0, KD, XW, 2 * XW))])
            load(K(C_QX), [((0, CW, KD), rows(win, 0, KD, COL_QX, COL_QX + 256))])
            for i, c0 in ((C_U, COL_U),):
                sp.wait_ge(lo_ready, i - RAW + 1)
                load(K(i), [((0, CW, KD), rows(win, 0, KD, c0, c0 + 256))])
            for kh in range(2):
                sp.wait_ge(lo_ready, C_V + kh - RAW + 1)
                load(K(C_V + kh), [((0, CW, 4), rows(win, 4 * kh, 4 * kh + 4, COL_V, COL_V + SBW))])
            for pr in range(HEADS // 2):
                sp.wait_ge(lo_ready, C_PAIR + pr - RAW + 1)
                load(K(C_PAIR + pr), [((0, 1024, KD), rows(win, 0, KD, pr * P, pr * P + P)),
                                      ((1024, 2048, KD), rows(win, 0, KD, COL_K + pr * P, COL_K + pr * P + P))])
            with sp.Fori(0, KD // 2) as dp:
                branch_col = sp.snap(dp * 256)
                for g in range(3):
                    c = K(C_MERGE + g, dp, PER_DP)
                    sp.wait_ge(lo_ready, upto(c, RAW))
                    col = COL_G + g * D
                    load(c, [((0, CW, KD), win[:, bass.ds(dp * 256 + col, 256)].rearrange("(k p) n -> p k n", p=P))])
                for j, (w, kk) in enumerate(((w_up_sb, 4), (w_up_pool, 2), (w_up_x, 2))):
                    c = K(C_MERGE + 3 + j, dp, PER_DP)
                    sp.wait_ge(lo_ready, upto(c, RAW))
                    sp.sem_inc(sp_free, 1)
                    load(c, [((0, kk * 256, kk), w[0][:, bass.ds(branch_col, 256)].rearrange("(k p) n -> p k n", p=P))])
            for i in range(4):
                half, kh = divmod(i, 2)
                sp.wait_ge(lo_ready, C_OUT + i - RAW + 1)
                load(K(C_OUT + i), [((0, CW, 4), rows(w_out[0], 4 * kh, 4 * kh + 4, half * 512, half * 512 + 512))])

            def expert_in(c, i, e):
                k0 = 2 * i * P
                load(c, [((0, CW // 2, 2), w_gate[0, e, k0:k0 + 2 * P, :].rearrange("(k p) n -> p k n", p=P)),
                         ((CW // 2, CW, 2), w_up[0, e, k0:k0 + 2 * P, :].rearrange("(k p) n -> p k n", p=P))])

            def expert_out(c, i, e):
                k0 = 2 * i * P
                load(c, [((0, CW, 2), w_down[0, e, k0:k0 + 2 * P, :].rearrange("(k p) n -> p k n", p=P))])

            def in_flight(c):
                c = K(c[0] - IN_FLIGHT, c[1], c[2])
                sp.sem_inc(sp_free, 1)
                sp.wait_ge(raw_slot(c)[1], raw_count(c))
                sp.sem_inc(sp_free, 1)

            for i in range(4):
                if i < RAW:
                    last = max(c for c in range(C_MOE) if c % RAW == i)
                    sp.wait_ge(lo_ready, last + 1)
                else:
                    after(sp, K(C_OUT - 1))
                expert_in(K(C_MOE + i), i, 0)
            for i in range(4):
                if i == 3:
                    sp.wait_ge(h2_out, 16 * TB)
                    sp.wait_ge(h2T_ps, TB)
                expert_in(K(C_MOE + 4 + i), i, 1)
            expert_out(K(C_MOE + 8), 0, 0)
            sp.wait_ge(lg_ps, 1)
            expert_out(K(C_MOE + 9), 1, 0)
            with sp.Fori(0, NE // 2 - 1) as j:
                for n in range(2):
                    e = sp.snap(j * 2 + n)
                    for i in range(4):
                        c = K(C_MOE + 10 + PER_E * n + i, j, RAW_MOE)
                        sp.wait_ge(lo_ready, upto(c, RAW_MOE))
                        in_flight(c)
                        if n == 0 and i == 1:
                            sp.wait_ge(route_ready, 1)
                        expert_in(c, i, e + 2)
                    for i in range(2):
                        c = K(C_MOE + 14 + PER_E * n + i, j, RAW_MOE)
                        sp.wait_ge(lo_ready, upto(c, RAW_MOE))
                        in_flight(c)
                        expert_out(c, i, e + 1)
            for i in range(2):
                c = K(C_OVER - 2 + i)
                sp.wait_ge(lo_ready, upto(c, RAW_MOE))
                expert_out(c, i, NE - 1)
            n_over = sp.value_load(tab[0:1, 0:1], min_val=0, max_val=OVER)
            with sp.Fori(0, OVER) as j:
                with sp.If(n_over > j):
                    e = sp.value_load(tab[0:1, bass.ds(j + 1, 1)], min_val=0, max_val=NE - 1)
                    for i in range(4):
                        c = K(C_OVER + i, j, PER_E)
                        sp.wait_ge(lo_ready, upto(c, RAW_OVER))
                        expert_in(c, i, e)
                    for i in range(2):
                        c = K(C_OVER + 4 + i, j, PER_E)
                        sp.wait_ge(lo_ready, upto(c, RAW_OVER))
                        expert_out(c, i, e)
                sp.nop()
            for t in range(TB):
                sp.wait_ge(res_ready, t + 1)
                sp.dma_start(out[0, t * P:(t + 1) * P, :], x2[:, t, :]).then_inc(out_done, 16)
            sp.wait_ge(out_done, 16 * TB)

        @block.gpsimd
        def _(pool):
            n_step = [0]

            def step(ins):
                n_step[0] += 1
                ins.then_inc(consts_mem, 1)
                pool.wait_ge(consts_mem, n_step[0])

            step(pool.memset(eps_c[:, :], EPS))
            step(pool.memset(ident[:, :], 0.0))
            step(pool.affine_select(out=ident[:, :], in_=ident[:, :], compare_op=ALU.not_equal, fill=1.0,
                                    base=0, pattern=[[-1, P]], channel_multiplier=1))
            step(pool.memset(tri_f[:, :], 0.0))
            step(pool.affine_select(out=tri_f[:, :], in_=tri_f[:, :], compare_op=ALU.is_gt, fill=-1.0,
                                    base=0, pattern=[[1, P]], channel_multiplier=-1))
            step(pool.memset(negmask[:, :], 0.0))
            step(pool.affine_select(out=negmask[:, :], in_=negmask[:, :], compare_op=ALU.is_gt, fill=NEG,
                                    base=0, pattern=[[1, P]], channel_multiplier=-1))
            step(pool.memset(rank_tri[:, :], 1.0))
            step(pool.affine_select(out=rank_tri[:, :], in_=rank_tri[:, :], compare_op=ALU.is_gt, fill=0.0,
                                    base=0, pattern=[[1, P]], channel_multiplier=-1))
            step(pool.memset(ones_b[:, :], 1.0))
            step(pool.iota(pos[:, :], pattern=[[1, 16]], base=1, channel_multiplier=0,
                           allow_small_or_imprecise_dtypes=True))
            step(pool.iota(jm[:, :], pattern=[[1, NE]], base=-64, channel_multiplier=0,
                           allow_small_or_imprecise_dtypes=True))
            step(pool.iota(e128[:, :], pattern=[[P, NE]], base=0, channel_multiplier=0,
                           allow_small_or_imprecise_dtypes=True))
            step(pool.memset(wp[:, :, :], 0.0))
            step(pool.iota(slot_no[:, :], pattern=[[1, P]], base=0, channel_multiplier=0))
            step(pool.iota(tile_no[:, :], pattern=[[1, SLOT_TILES]], base=0, channel_multiplier=0))
            step(pool.iota(id_block[:, :], pattern=[[0, 2], [2 * P, TB]], base=-NO_ROW, channel_multiplier=0,
                           allow_small_or_imprecise_dtypes=True))
            step(pool.iota(id_row[:, :], pattern=[[1, 2], [0, TB]], base=0, channel_multiplier=2,
                           allow_small_or_imprecise_dtypes=True))
            pool.sem_inc(consts_ready, 1)
            pool.sem_inc(ye_free, 2)
            for g in range(4):
                lo = DH * (g % 2)
                pool.dma_start(wp[lo:lo + DH, g // 2, lo:lo + DH], w_pool[0, g]).then_inc(small_in, 16)
            pool.dma_start(wr[:, :, 0:NG], w_group[0].rearrange("(k p) n -> p k n", p=P)).then_inc(small_in, 16)
            pool.dma_start(wr[:, :, NG:NG + NE], w_router[0].rearrange("(k p) n -> p k n", p=P)).then_inc(small_in, 16)
            pool.dma_start(bias_bc[:, 0:NG], b_group[0:1, :].broadcast_to([P, NG])).then_inc(small_in, 16)
            pool.dma_start(bias_bc[:, NG:NG + NE], b_router[0:1, :].broadcast_to([P, NE])).then_inc(small_in, 16)
            pool.wait_ge(b_used, 3)
            pool.dma_start(gffn_bc[:, :], norm_ffn[0:1, :].broadcast_to([P, D])).then_inc(gffn_in, 16)
            after(pool, K(C_OUT - 1))
            pool.dma_start(x2[:, :, :], x[0].rearrange("(t p) d -> p t d", p=P)).then_inc(xres_in, 16)
            for t in range(TB):
                pool.wait_ge(h2_ready, t + 1)
                pool.dma_start(h2_rows[t * P:(t + 1) * P, :], h2[:, t, :]).then_inc(h2_out, 16)
            after(pool, K(C_OUT + 3))
            for b in range(2):
                pool.memset(xe[b][:, :], 0.0).then_inc(xe_clear, 1)
            pool.wait_ge(xe_clear, 2)
            pool.wait_ge(h2_out, 16 * TB)
            pool.wait_ge(rows_ready, 1)

            def x_load(tile, b, n):
                if n is not None:
                    pool.wait_ge(xe_ps, n)
                    pool.sem_inc(pool_free, 1)
                pool.tensor_copy(x_col[b][:, :], x_row[:, bass.ds(tile, 1)]).then_inc(x_col_set, 1)
                pool.wait_ge(x_col_set, tile + 1)
                pool.sem_inc(pool_free, 1)
                pool.indirect_dma_start(xe[b][:, :], None, h2_rows[:, :],
                                        bass.IndirectOffsetOnAxis(x_col[b][:, :].bitcast(U32), 0),
                                        bounds_check=S - 1, oob_is_err=False).then_inc(xe_in[b], 16)

            def y_store(tile, b, before):
                pool.wait_ge(y_a, tile + 1)
                pool.wait_ge(y_v, tile + 1)
                pool.sem_inc(pool_free, 1)
                pool.tensor_copy(y_col[b][:, :], y_row[:, bass.ds(tile, 1)]).then_inc(y_col_set, 1)
                pool.wait_ge(y_col_set, tile + 1)
                pool.sem_inc(pool_free, 1)
                pool.indirect_dma_start(y_rows[:, :], bass.IndirectOffsetOnAxis(y_col[b][:, :].bitcast(U32), 0),
                                        ye[b][:, :], None, bounds_check=2 * S - 1, oob_is_err=False).then_inc(y_out[b], 16)
                if before is not None:
                    pool.wait_ge(y_out[1 - b], 16 * before)
                    pool.sem_inc(ye_free, 1)

            x_load(0, 0, None)
            x_load(1, 1, None)
            pool.dma_start(gfin_bc[:, :], norm_final.rearrange("(a d) -> a d", a=1).broadcast_to([P, D])).then_inc(gfin_in, 16)
            x_load(2, 0, 1)
            x_load(3, 1, 2)
            y_store(0, 0, None)
            with pool.Fori(0, NE // 2 - 2) as j:
                for n in range(2):
                    step = pool.snap(j * 2 + n)
                    x_load(step + 4, n, step + 3)
                    y_store(step + 1, (n + 1) % 2, j + 1)
            x_load(NE, 0, NE - 1)
            for tile in range(NE - 3, NE):
                y_store(tile, tile % 2, (tile + 1) // 2)
            pool.wait_ge(route_ready, 1)
            n_over = pool.value_load(tab[0:1, 0:1], min_val=0, max_val=OVER)
            with pool.Fori(0, OVER) as j:
                with pool.If(n_over > j):
                    x_load(j + NE + 1, 0, j + NE + 1)
                    y_store(j + NE, 0, None)
                    pool.wait_ge(y_out[0], (j + NE // 2 + 1) * 16)
                    pool.sem_inc(ye_free, 1)
                pool.nop()
            pool.wait_ge(y_out[1], NE // 2 * 16)
            for t in range(TB):
                pool.dma_start(y_in[:, t, :, :], y_rows[2 * t * P:2 * (t + 1) * P, :].rearrange("(p r) d -> p r d", r=2)) \
                    .then_inc(y_back[t], 16)

        @block.scalar
        def _(act):
            def root(cols, n):
                act.wait_ge(ss_ready, n)
                act.activation(std[:, cols], ss[:, cols], ACT.Sqrt, scale=1.0 / D, bias=eps_c[:, :]) \
                   .then_inc(std_ready, cols.stop - cols.start)

            act.wait_ge(mem_in, 16)
            for b in range(MB):
                if b:
                    act.wait_ge(ss_ready, b)
                act.activation(junk[:, :], memn[:, b, :], ACT.Square, accum_out=ss[:, b:b + 1]).then_inc(ss_ready, 1)
            act.wait_ge(consts_ready, 1)
            root(slice(0, MB), MB)
            split_hi(act, K(0))
            for t in range(TB):
                act.wait_ge(x_in[t], 16)
                act.wait_ge(ss_ready, MB + t)
                act.activation(junk[:, :], xn[:, t, :], ACT.Square, accum_out=ss[:, MB + t:MB + t + 1]).then_inc(ss_ready, 1)
            root(slice(MB, MB + TB), MB + TB)
            split_hi(act, K(1))
            act.activation(negtri[:, :], tri_f[:, :], ACT.Copy).then_inc(consts_r, 1)
            act.activation(negones[:, :], ones_b[:, :], ACT.Copy, scale=-1.0).then_inc(consts_r, 1)
            act.activation(identb[:, :], ident[:, :], ACT.Copy).then_inc(consts_r, 1)
            act.wait_ge(gains_ready, 1)
            for b in range(4):
                act.wait_ge(memT_ps, b + 1)
                for k in (2 * b, 2 * b + 1):
                    act.activation(memT_hi[:, k, :], bank(b)[:, (k % 2) * MEM:(k % 2 + 1) * MEM], ACT.Copy,
                                   scale=gains[:, KD + k:KD + k + 1]).then_inc(memT_h, 1)
            for k in range(KD):
                act.wait_ge(hT_ps, k + 1)
                act.activation(hT_hi[:, k, :], bank(4 + k % 4), ACT.Copy,
                               scale=gains[:, k:k + 1]).then_inc(hT_h, 1)

            def proj_hi(n, ahead, dst, src):
                if ahead is not None:
                    split_hi(act, K(ahead))
                if dst is not None:
                    after(act, K((C_KM, C_VM, C_QX, C_U, C_V + 1)[n - 1]))
                    act.activation(dst, src, ACT.Copy).then_inc(proj_h, 1)

            proj_hi(1, C_KM + 2, km_hi[:, :, :], bank(0))
            proj_hi(2, C_VM + 2, vm_hi[:, :, :], bank(1))
            proj_hi(3, C_QX + 2, qx_hi[:, :, :], bank(2, 2))
            proj_hi(4, C_U + 2, None, None)

            def qk_hi(n, b):
                if n % 2:
                    after(act, K(C_PAIR + n // 2))
                else:
                    act.wait_ge(q_ps, n // 2 + 1)
                dst = (k_hi if n % 2 else q_hi)[:, n // 2 % 2, :]
                act.activation(dst, bank(b), ACT.Copy, scale=1.0 if n % 2 else SCALE).then_inc(qk_h, 1)

            def cross_exp(r):
                act.wait_ge(xs_max, r + 1)
                if r == 0:
                    act.wait_ge(pool_d, 2)
                else:
                    act.wait_ge(xt_ps, r)
                for i in range(8):
                    ins = act.activation(probs[:, i, :], bank(4, 4)[:, i * MEM:(i + 1) * MEM], ACT.Exp,
                                         bias=nmx[:, r, i:i + 1], scale=SCALE, accum_out=den[:, r, i:i + 1])
                ins.then_inc(xs_exp, 1)

            def cross_t(r):
                act.wait_ge(xt_ps, r + 1)
                if r > 0:
                    act.wait_ge(xo_ps, r)
                act.activation(pT_hi[:, :, :], bank(4, 4), ACT.Copy).then_inc(xt_h, 1)

            def cross_o(r):
                act.wait_ge(xo_ps, r + 1)
                for h in range(2):
                    rows = slice(DH * h, DH * h + DH)
                    ins = act.activation(xaT_hi[rows, r, :], bank(6 * r + h)[rows, :], ACT.Copy)
                ins.then_inc(xo_h, 1)

            act.preload_act_table_set("natural_log_exp_and_others")
            cross_exp(0)
            proj_hi(5, C_PAIR, v_hi[:, :, :], bank(0, 4))
            split_hi(act, K(C_PAIR + 1))
            act.wait_ge(pool_ps, 1)
            for c in range(2):
                act.activation(plT_hi[:, c, :], bank(c), ACT.Copy,
                               scale=gains[:, 2 * KD + c:2 * KD + c + 1]).then_inc(pool_h, 1)
            cross_t(0)
            qk_hi(0, 2)
            qk_hi(1, 3)
            cross_o(0)
            split_hi(act, K(C_PAIR + 2))
            cross_exp(1)
            qk_hi(2, 2)
            qk_hi(3, 3)
            split_hi(act, K(C_PAIR + 3))
            cross_t(1)

            def scores(n):
                return bank(3 * (n % 2), 3)[:, 0:ZW]

            def logarithm(n):
                act.wait_ge(z_ps, n + 1)
                if n > 0:
                    act.wait_ge(z_soft, n)
                act.activation(log_in[:, :], scores(n), ACT.Abs).then_inc(act_c, 1)
                act.wait_ge(act_c, 2 * n + 1)
                act.activation(log_in[:, :], log_in[:, :], ACT.Exp, scale=-1.0).then_inc(act_c, 1)
                act.wait_ge(act_c, 2 * n + 2)
                act.activation(log_in[:, :], log_in[:, :], ACT.Ln, bias=1.0).then_inc(z_ln, 1)

            logarithm(0)
            cross_o(1)
            split_hi(act, K(C_MERGE))
            for n in range(HEADS + 2):
                if n >= 2:
                    m = n - 2
                    rows = slice(DH * (m % 2), DH * (m % 2) + DH)
                    act.wait_ge(av_ps, m + 1)
                    act.activation(sbT_hi[rows, m // 2, :], bank(7)[rows, :], ACT.Copy).then_inc(av_h, 1)
                if n < HEADS:
                    act.wait_ge(z_soft, n + 1)
                    act.activation(soft_hi[:, :], soft[:, :], ACT.Copy).then_inc(soft_h, 1)
                if n + 1 < HEADS:
                    logarithm(n + 1)
                if 1 <= n <= 4:
                    qk_hi(n + 3, 6)
                if n < HEADS:
                    act.wait_ge(tail_ps, n + 1)
                    if n >= 2:
                        act.wait_ge(av_ps, n - 1)
                    act.activation(attn[n % 2][:, :], scores(n), ACT.Exp).then_inc(a_exp, 1)
                if n == HEADS - 1:
                    split_hi(act, K(C_MERGE + 1))

            act.preload_act_table_set("sigmoid_and_others")
            with act.Fori(0, KD // 2) as dp:
                for i in range(PER_DP):
                    split_hi(act, K(C_MERGE + i + 2, dp, PER_DP), width_of(C_MERGE + (i + 2) % PER_DP))
                    if i < 3:
                        after(act, K(C_MERGE + i, dp, PER_DP))
                        act.activation(sig[:, i, :, :], bank(2 * i, 2), ACT.Sigmoid).then_inc(g_sig, 1)
                act.wait_ge(mg_ready, dp + 1)
                act.activation(mgT_hi[:, bass.ds(dp * 2, 2), :], merged[:, :, :], ACT.Copy).then_inc(mg_h, 1)
            act.preload_act_table_set("sqrt_and_others")
            for i in range(3):
                split_hi(act, K(C_OUT + i + 2))

            for t in range(TB + 1):
                if t < TB:
                    act.wait_ge(x2_ready, t + 1)
                    act.wait_ge(ss_ready, MB + TB + t)
                    act.activation(junk2[:, :], x2[:, t, :], ACT.Square, accum_out=ss[:, 8 + t:9 + t]).then_inc(ss_ready, 1)
                    root(slice(8 + t, 9 + t), MB + TB + t + 1)
                if t >= 1:
                    act.wait_ge(h2T_ps, t)
                    act.activation(h2T[:, t - 1, 0:4, :], bank(2 * ((t - 1) % 2)), ACT.Copy).then_inc(h2T_a, 1)
            split_hi(act, K(C_MOE + 1))
            split_hi(act, K(C_MOE + 2))
            act.wait_ge(r_max, 1)
            act.activation(ex[:, :, 0:5], ex[:, :, 0:5], ACT.Exp).then_inc(r_exp, 1)
            act.preload_act_table_set("silu_and_others")

            def xe_hi(n):
                act.wait_ge(xe_ps, n)
                act.activation(xT_hi[:, :], bank(2, 2), ACT.Copy).then_inc(xe_h, 1)

            def silu(c):
                after(act, c)
                act.activation(silu_g[:, :], bank(0), ACT.Silu).then_inc(silu_ready, 1)

            def aT_h(n):
                act.wait_ge(at_ps, n)
                act.activation(aT_hi[:, :], bank(4), ACT.Copy).then_inc(at_h, 1)

            def y_half(c, b, free):
                after(act, c)
                act.wait_ge(ye_free, free)
                act.activation(ye[b][:, 0:512], bank(5), ACT.Copy).then_inc(y_a, 1)

            xe_hi(1)
            for i in range(4):
                if i > 0:
                    split_hi(act, K(C_MOE + i + 2))
            silu(K(C_MOE + 3))
            xe_hi(2)
            for i in range(PER_E):
                split_hi(act, K(C_MOE + 4 + i + 2))
                if i == 1:
                    aT_h(1)
                if i == 3:
                    silu(K(C_MOE + 7))
                    xe_hi(3)
            with act.Fori(0, NE // 2 - 1) as j:
                for n in range(2):
                    step = act.snap(j * 2 + n)
                    for i in range(PER_E):
                        split_hi(act, K(C_MOE + 10 + PER_E * n + i + 2, j, RAW_MOE))
                        if i == 0:
                            y_half(K(C_MOE + 9 + PER_E * n, j, RAW_MOE), n, step + 1)
                        if i == 1:
                            aT_h(step + 2)
                        if i == 3:
                            silu(K(C_MOE + 13 + PER_E * n, j, RAW_MOE))
                            xe_hi(step + 4)
            y_half(K(C_OVER - 3), 0, NE - 1)
            aT_h(NE)
            y_half(K(C_OVER - 1), 1, NE)
            act.wait_ge(route_ready, 1)
            n_over = act.value_load(tab[0:1, 0:1], min_val=0, max_val=OVER)
            with act.Fori(0, OVER) as j:
                with act.If(n_over > j):
                    for i in range(PER_E):
                        split_hi(act, K(C_OVER + i, j, PER_E))
                    silu(K(C_OVER + 3, j, PER_E))
                    xe_hi(j + NE + 2)
                    aT_h(j + NE + 1)
                    y_half(K(C_OVER + 5, j, PER_E), 0, j + NE + 1)
                act.nop()
            act.preload_act_table_set("sqrt_and_others")
            for t in range(TB):
                act.wait_ge(comb_ready, t + 1)
                act.wait_ge(ss_ready, MB + 2 * TB + t)
                act.activation(junk3[:, :], x2[:, t, :], ACT.Square, accum_out=ss[:, 12 + t:13 + t]).then_inc(ss_ready, 1)
                root(slice(12 + t, 13 + t), MB + 2 * TB + t + 1)

        @block.tensor
        def _(pe):
            def chunk(c):
                pe.wait_ge(lo_ready, upto(c))
                s = c[0] % SPLIT
                return ring_hi[:, s, :], ring_lo[:, s, :]

            pe.wait_ge(consts_ready, 1)
            pe.wait_ge(gain_in, 48)
            pe.transpose(bank(7)[:, 0:2 * KD + 2], gain_rows[:, :], ident[0:2 * KD + 2, 0:2 * KD + 2]).then_inc(gains_ps, 1)
            for b in range(4):
                if b == 0:
                    pe.wait_ge(xn_ready, MB)
                for k in (2 * b, 2 * b + 1):
                    for m in range(MB):
                        o = (k % 2) * MEM + m * P
                        ins = pe.transpose(bank(b)[:, o:o + P], memn[:, m, k * P:(k + 1) * P], ident[:, :])
                ins.then_inc(memT_ps, 1)
            pe.wait_ge(xn_ready, MB + TB)
            pe.wait_ge(gains_ready, 1)
            for k in range(KD):
                if k >= 4:
                    pe.wait_ge(hT_l, k - 3)
                for t in range(TB):
                    ins = pe.transpose(bank(4 + k % 4)[:, t * P:(t + 1) * P], xn[:, t, k * P:(k + 1) * P], ident[:, :])
                ins.then_inc(hT_ps, 1)

            pe.wait_ge(memT_l, KD)
            wh, wl = chunk(K(C_KM))
            for c in range(2):
                for k in range(KD):
                    o = k * 256 + c * P
                    ins = three(pe, bank(0)[:, c * MEM:(c + 1) * MEM], wh[:, o:o + P], wl[:, o:o + P],
                                memT_hi[:, k, :], memT_lo[:, k, :], k == 0, k == KD - 1)
            ins.then_inc(chunk_used, 1)
            wh, wl = chunk(K(C_VM))
            for m in range(MB):
                for k in range(KD):
                    ins = three(pe, bank(1)[:, m * XW:(m + 1) * XW], memT_hi[:, k, m * P:(m + 1) * P],
                                memT_lo[:, k, m * P:(m + 1) * P], wh[:, k * 256:(k + 1) * 256],
                                wl[:, k * 256:(k + 1) * 256], k == 0, k == KD - 1)
            ins.then_inc(chunk_used, 1)

            def proj(b, wh, wl, o0, step):
                for k in range(KD):
                    o = o0 + k * step
                    ins = three(pe, bank(b), wh[:, o:o + P], wl[:, o:o + P], hT_hi[:, k, :], hT_lo[:, k, :],
                                k == 0, k == KD - 1)
                return ins

            pe.wait_ge(hT_l, KD)
            wh, wl = chunk(K(C_QX))
            proj(2, wh, wl, 0, 256)
            proj(3, wh, wl, P, 256).then_inc(chunk_used, 1)
            wh, wl = chunk(K(C_U))
            proj(4, wh, wl, 0, 256)
            proj(5, wh, wl, P, 256).then_inc(chunk_used, 1)
            def cross_scores(r):
                if r == 0:
                    pe.wait_ge(proj_l, 3)
                    pe.wait_ge(pool_d, 1)
                else:
                    pe.wait_ge(xt_l, r)
                for h in range(2):
                    rows = slice(DH * h, DH * h + DH)
                    for t in range(TB):
                        o = (h * TB + t) * MEM
                        ins = three(pe, bank(4, 4)[:, o:o + MEM], qx_hi[rows, r, t * P:(t + 1) * P],
                                    qx_lo[rows, r, t * P:(t + 1) * P], km_hi[rows, r, :], km_lo[rows, r, :],
                                    True, True)
                ins.then_inc(xs_ps, 1)

            def cross_transpose(r):
                pe.wait_ge(xs_norm, r + 1)
                for h in range(2):
                    for m in range(MB):
                        for t in range(TB):
                            ins = pe.transpose(bank(4 + 2 * h + m)[:, t * P:(t + 1) * P],
                                               probs[:, h * TB + t, m * P:(m + 1) * P], ident[:, :])
                ins.then_inc(xt_ps, 1)

            def cross_out(r):
                pe.wait_ge(xt_l, r + 1)
                if r == 0:
                    pe.wait_ge(pool_l, 2)
                for h in range(2):
                    for m in range(MB):
                        ins = three(pe, bank(6 * r + h), vm_hi[:, m, r * P:(r + 1) * P], vm_lo[:, m, r * P:(r + 1) * P],
                                    pT_hi[:, 2 * h + m, :], pT_lo[:, 2 * h + m, :], m == 0, m == MB - 1)
                ins.then_inc(xo_ps, 1)

            def project_qk(n, b):
                wh, wl = chunk(K(C_PAIR + n // 2))
                if n >= 4:
                    pe.wait_ge(z_ps, n - 2)
                proj(b, wh, wl, 1024 * (n % 2), P).then_inc(chunk_used if n % 2 else q_ps, 1)

            cross_scores(0)
            for kh in range(2):
                wh, wl = chunk(K(C_V + kh))
                for kk in range(4):
                    for t in range(TB):
                        k = 4 * kh + kk
                        ins = three(pe, bank(t), hT_hi[:, k, t * P:(t + 1) * P], hT_lo[:, k, t * P:(t + 1) * P],
                                    wh[:, kk * 512:(kk + 1) * 512], wl[:, kk * 512:(kk + 1) * 512],
                                    k == 0, k == KD - 1)
                ins.then_inc(chunk_used, 1)
            cross_transpose(0)
            pe.wait_ge(pool_d, 2)
            pe.wait_ge(proj_l, 4)
            pe.wait_ge(small_in, 16 * 8)
            for c in range(2):
                ins = pe.matmul(bank(c), wp[:, c, :], pool_a[:, c, U0:], start=True, stop=True)
            ins.then_inc(pool_ps, 1)
            project_qk(0, 2)
            project_qk(1, 3)
            cross_out(0)
            cross_scores(1)
            pe.wait_ge(qk_l, 1)
            project_qk(2, 2)
            pe.wait_ge(qk_l, 2)
            project_qk(3, 3)
            cross_transpose(1)

            def scores(n):
                rows = slice(DH * (n % 2), DH * (n % 2) + DH)
                pe.wait_ge(qk_l, 2 * (n // 2) + 2)
                if n == 0:
                    pe.wait_ge(xo_l, 1)
                    pe.wait_ge(qk_l, 3)
                if n == 1:
                    pe.wait_ge(qk_l, 4)
                    pe.wait_ge(xt_l, 2)
                if n >= 2:
                    pe.wait_ge(a_exp, n - 1)
                zz = bank(3 * (n % 2), 3)
                for sbk in (0, 1, 3, 2):
                    keys = slice(sbk * P, sbk * P + P)
                    o, w = ZOFF[sbk], ZN[sbk]
                    first = sbk != 3
                    three(pe, zz[:, o:o + w], k_hi[rows, n // 2 % 2, keys], k_lo[rows, n // 2 % 2, keys],
                          q_hi[rows, n // 2 % 2, sbk * P:], q_lo[rows, n // 2 % 2, sbk * P:], first, False)
                    ins = pe.matmul(zz[:, o:o + P], identb[:, :], negmask[:, :], start=False, stop=True,
                                    skip_group_check=True)
                ins.then_inc(z_ps, 1)

            def tails(n):
                pe.wait_ge(soft_l, n + 1)
                zz = bank(3 * (n % 2), 3)
                for sbk in range(TB):
                    for jb in range(sbk, TB):
                        o = ZOFF[sbk] + (jb - sbk) * P
                        j, w = ZOFF[jb], ZN[jb]
                        lhs = negtri if jb == sbk else negones
                        pe.matmul(zz[:, o:o + w], lhs[:, :], soft_hi[:, j:j + w], start=False, stop=False,
                                  skip_group_check=True)
                        ins = pe.matmul(zz[:, o:o + w], lhs[:, :], soft_lo[:, j:j + w], start=False,
                                        stop=jb == TB - 1, skip_group_check=True)
                ins.then_inc(tail_ps, 1)

            def values(m):
                pr = m // 2
                pe.wait_ge(a_l, m + 1)
                if m >= 1:
                    pe.wait_ge(av_l, m)
                for sbk in range(TB):
                    o, w = ZOFF[sbk], ZN[sbk]
                    ins = three(pe, bank(7)[:, sbk * P:], v_hi[:, sbk, pr * P:(pr + 1) * P],
                                v_lo[:, sbk, pr * P:(pr + 1) * P], attn_hi[:, o:o + w], attn_lo[m % 2][:, o:o + w],
                                sbk == 0, sbk == TB - 1)
                ins.then_inc(av_ps, 1)

            scores(0)
            cross_out(1)
            scores(1)
            pe.wait_ge(xo_l, 2)
            branches = ((sbT_hi, sbT_lo, 4), (plT_hi, plT_lo, 2), (xaT_hi, xaT_lo, 2))

            def gate(g, d, dp):
                wh, wl = chunk(K(C_MERGE + PER_DP * d + g, dp, PER_DP))
                proj(2 * g, wh, wl, 0, 256)
                proj(2 * g + 1, wh, wl, P, 256).then_inc(chunk_used, 1)

            for n in range(HEADS + 1):
                if n < HEADS:
                    tails(n)
                else:
                    pe.wait_ge(a_exp, HEADS - 1)
                    gate(0, 0, None)
                if n >= 1:
                    values(n - 1)
                if n + 2 < HEADS:
                    scores(n + 2)
                if n < 4:
                    if n >= 1:
                        pe.wait_ge(qk_l, n + 4)
                    project_qk(n + 4, 6)

            pe.wait_ge(av_l, HEADS)
            pe.wait_ge(xo_l, 2)
            pe.wait_ge(pool_l, 2)

            def rest(d, dp):
                done = 3 * d if dp is None else dp * 3 + 3 * d
                for g in (1, 2):
                    pe.wait_ge(b_used, done + g + 1)
                    gate(g, d, dp)
                for j, (bh, bl, kk) in enumerate(branches):
                    pe.wait_ge(g_sig, done + j + 1)
                    wh, wl = chunk(K(C_MERGE + PER_DP * d + 3 + j, dp, PER_DP))
                    for c in range(2):
                        for k in range(kk):
                            o = k * 256 + c * P
                            ins = three(pe, bank(2 * j + c), wh[:, o:o + P], wl[:, o:o + P], bh[:, k, :], bl[:, k, :],
                                        k == 0, k == kk - 1)
                    ins.then_inc(chunk_used, 1)

            with pe.Fori(0, KD // 2 - 1) as dp:
                rest(0, dp)
                pe.wait_ge(b_used, dp * 3 + 4)
                gate(0, 1, dp)
            rest(KD // 2 - 1, None)

            pe.wait_ge(mg_l, KD // 2 - 1)
            pe.wait_ge(b_used, 2 + 3 * (KD // 2))
            for kh in range(2):
                wh, wl = chunk(K(C_OUT + kh))
                for kk in range(4):
                    k = 4 * kh + kk
                    if k == KD - 2:
                        pe.wait_ge(mg_l, KD // 2)
                    for t in range(TB):
                        ins = three(pe, bank(t), mgT_hi[:, k, t * P:(t + 1) * P],
                                    mgT_lo[:, k, t * P:(t + 1) * P], wh[:, kk * 512:(kk + 1) * 512],
                                    wl[:, kk * 512:(kk + 1) * 512], k == 0, k == KD - 1)
                ins.then_inc(chunk_used, 1)

            out_w = [chunk(K(C_OUT + 2 + kh)) for kh in range(2)]

            pe.wait_ge(b_used, 3 + 3 * (KD // 2))

            def out_block(t):
                for k in range(KD):
                    wh, wl = out_w[k // 4]
                    n0 = (k % 4) * 512
                    ins = three(pe, bank(4 + t), mgT_hi[:, k, t * P:(t + 1) * P], mgT_lo[:, k, t * P:(t + 1) * P],
                                wh[:, n0:n0 + 512], wl[:, n0:n0 + 512], k == 0, k == KD - 1)
                    if t == TB - 1 and k % 4 == 3:
                        ins.then_inc(chunk_used, 1)
                if t < TB - 1:
                    ins.then_inc(o_ps, 1)

            def h2_transpose(t):
                pe.wait_ge(h2_ready, t + 1)
                if t == 0:
                    pe.wait_ge(x2_half, 1)
                if t >= 2:
                    pe.wait_ge(h2T_a, t - 1)
                    pe.wait_ge(h2T_v, t - 1)
                for k in range(KD):
                    ins = pe.transpose(bank(2 * (t % 2), 2)[:, k * P:(k + 1) * P], h2[:, t, k * P:(k + 1) * P], ident[:, :])
                ins.then_inc(h2T_ps, 1)

            def logits(t):
                if t == 0:
                    pe.wait_ge(x2_ready, 1)
                    pe.wait_ge(small_in, 16 * 8)
                pe.wait_ge(h2T_a, t + 1)
                pe.wait_ge(h2T_v, t + 1)
                for k in range(KD):
                    ins = pe.matmul(bank(4)[:, t * (NG + NE):(t + 1) * (NG + NE)], h2T[:, t, k, :],
                                    wr[:, k, :], start=k == 0, stop=k == KD - 1)
                if t == TB - 1:
                    ins.then_inc(lg_ps, 1)

            out_block(0)
            out_block(1)
            out_block(2)
            h2_transpose(0)
            out_block(3)
            h2_transpose(1)
            logits(0)
            h2_transpose(2)
            logits(1)
            h2_transpose(3)
            logits(2)
            logits(3)
            pe.wait_ge(onehot_ready, 1)
            for t in range(TB):
                for u in range(t + 1):
                    pe.matmul(bank(5)[:, t * NE:(t + 1) * NE], (rank_tri if u == t else ones_b)[:, :],
                              onehot_b[:, u, :], start=u == 0, stop=u == t)
            for u in range(TB):
                ins = pe.matmul(bank(5)[:, TB * NE:(TB + 1) * NE], ones_b[:, :], onehot_b[:, u, :],
                                start=u == 0, stop=u == TB - 1)
            ins.then_inc(rank_ps, 1)
            for c in range(2 * TB):
                if c % TB == 0:
                    pe.wait_ge(sel_ready, c // TB + 1)
                pe.matmul(bank(6)[:, 0:SLOT_TILES], at_part[:, c, :], at_block[:, c, :], start=c == 0, stop=False)
                ins = pe.matmul(bank(6)[:, 0:SLOT_TILES], at_part[:, c, :], at_row[:, c, :],
                                start=False, stop=c == 2 * TB - 1)
            ins.then_inc(rows_ps, 1)

            def x_transpose(n, b, loads, read):
                pe.wait_ge(xe_in[b], loads * 16)
                if read is not None:
                    pe.wait_ge(xe_l, read)
                for k in range(KD):
                    ins = pe.transpose(bank(2, 2)[:, k * P:(k + 1) * P], xe[b][:, k * P:(k + 1) * P], ident[:, :])
                ins.then_inc(xe_ps, 1)

            def gate_up(n, c0, i, j, before, per=RAW_MOE):
                if i == 0:
                    pe.wait_ge(xe_l, n)
                    if before is not None:
                        pe.wait_ge(act_ready, before)
                wh, wl = chunk(K(c0 + i, j, per))
                for kk in range(2):
                    k = 2 * i + kk
                    for u in range(2):
                        o = u * 1024 + kk * 512
                        ins = three(pe, bank(u), xT_hi[:, k * P:(k + 1) * P], xT_lo[:, k * P:(k + 1) * P],
                                    wh[:, o:o + 512], wl[:, o:o + 512], k == 0, k == KD - 1)
                ins.then_inc(chunk_used, 1)

            def a_transpose(n, read):
                pe.wait_ge(act_ready, n)
                if read is not None:
                    pe.wait_ge(at_l, read)
                for f in range(4):
                    ins = pe.transpose(bank(4)[:, f * P:(f + 1) * P], act_e[:, f * P:(f + 1) * P], ident[:, :])
                ins.then_inc(at_ps, 1)

            def down(n, c0, j, read, per=RAW_MOE):
                pe.wait_ge(at_l, n)
                if read is not None:
                    pe.wait_ge(y_a, read)
                    pe.wait_ge(y_v, read)
                for i in range(2):
                    wh, wl = chunk(K(c0 + i, j, per))
                    for kk in range(2):
                        f = 2 * i + kk
                        for half in range(2):
                            o = kk * 1024 + half * 512
                            ins = three(pe, bank(5 + half), aT_hi[:, f * P:(f + 1) * P], aT_lo[:, f * P:(f + 1) * P],
                                        wh[:, o:o + 512], wl[:, o:o + 512], f == 0, f == 3)
                    ins.then_inc(chunk_used, 1)

            x_transpose(1, 0, 1, None)
            for i in range(4):
                gate_up(1, C_MOE, i, None, None)
            x_transpose(2, 1, 1, 1)
            for i in range(4):
                gate_up(2, C_MOE + 4, i, None, 1)
                if i == 1:
                    a_transpose(1, None)
            x_transpose(3, 0, 2, 2)
            down(1, C_MOE + 8, None, None)
            with pe.Fori(0, NE // 2 - 1) as j:
                for n in range(2):
                    step = pe.snap(j * 2 + n)
                    for i in range(4):
                        gate_up(step + 3, C_MOE + 10 + PER_E * n, i, j, step + 2)
                        if i == 1:
                            a_transpose(step + 2, step + 1)
                    x_transpose(step + 4, (n + 1) % 2, j + 2 + n, step + 3)
                    down(step + 2, C_MOE + 14 + PER_E * n, j, step + 1)
            a_transpose(NE, NE - 1)
            down(NE, C_OVER - 2, None, NE - 1)
            pe.wait_ge(route_ready, 1)
            n_over = pe.value_load(tab[0:1, 0:1], min_val=0, max_val=OVER)
            with pe.Fori(0, OVER) as j:
                with pe.If(n_over > j):
                    for i in range(4):
                        gate_up(j + NE + 1, C_OVER, i, j, j + NE, PER_E)
                    x_transpose(j + NE + 2, 0, j + NE // 2 + 2, j + NE + 1)
                    a_transpose(j + NE + 1, j + NE)
                    down(j + NE + 1, C_OVER + 4, j, j + NE, PER_E)
                pe.nop()

        @block.vector
        def _(dve):
            n_link = [0]

            def link(ins):
                n_link[0] += 1
                ins.then_inc(dve_c, 1)
                dve.wait_ge(dve_c, n_link[0])

            def rsqrt(cols, n):
                dve.wait_ge(ss_ready, n)
                link(dve.tensor_scalar(ms[:, cols], ss[:, cols], 1.0 / D, EPS, ALU.mult, ALU.add))
                dve.wait_ge(std_ready, n)
                link(dve.reciprocal(rstd[:, cols], std[:, cols]))
                link(dve.tensor_tensor(ms[:, cols], ms[:, cols], rstd[:, cols], ALU.mult))
                link(dve.tensor_tensor(ms[:, cols], ms[:, cols], rstd[:, cols], ALU.mult))
                link(dve.tensor_scalar(ms[:, cols], ms[:, cols], -0.5, 1.5, ALU.mult, ALU.add))
                link(dve.tensor_tensor(rstd[:, cols], rstd[:, cols], ms[:, cols], ALU.mult))

            rsqrt(slice(0, MB), MB)
            for b in range(MB):
                dve.tensor_scalar(memn[:, b, :], memn[:, b, :], rstd[:, b:b + 1], None, ALU.mult).then_inc(xn_ready, 1)
            split_lo(dve, K(0))
            dve.wait_ge(gains_ps, 1)
            dve.tensor_copy(gains[:, :], bank(7)[:, 0:2 * KD + 2]).then_inc(gains_ready, 1)
            rsqrt(slice(MB, MB + TB), MB + TB)
            for t in range(TB):
                dve.tensor_scalar(xn[:, t, :], xn[:, t, :], rstd[:, MB + t:MB + t + 1], None, ALU.mult).then_inc(xn_ready, 1)
            split_lo(dve, K(1))
            dve.wait_ge(gains_ready, 1)
            for b in range(4):
                dve.wait_ge(memT_h, 2 * b + 2)
                for k in (2 * b, 2 * b + 1):
                    dve.scalar_tensor_tensor(memT_lo[:, k, :], bank(b)[:, (k % 2) * MEM:(k % 2 + 1) * MEM],
                                             gains[:, KD + k:KD + k + 1], memT_hi[:, k, :].bitcast(F32),
                                             ALU.mult, ALU.subtract).then_inc(memT_l, 1)
            for k in range(KD):
                dve.wait_ge(hT_h, k + 1)
                dve.scalar_tensor_tensor(hT_lo[:, k, :], bank(4 + k % 4), gains[:, k:k + 1],
                                         hT_hi[:, k, :].bitcast(F32), ALU.mult, ALU.subtract).then_inc(hT_l, 1)

            def less(dst, src, hi):
                return dve.tensor_tensor(dst, src, hi.bitcast(F32), ALU.subtract)

            def flat(ap):
                return ap.rearrange("p a b -> p (a b)")

            split_lo(dve, K(C_KM + 2))
            dve.wait_ge(proj_h, 1)
            less(flat(km_lo[:, :, :]), bank(0), flat(km_hi[:, :, :])).then_inc(proj_l, 1)
            split_lo(dve, K(C_VM + 2))
            dve.wait_ge(proj_h, 2)
            less(flat(vm_lo[:, :, :]), bank(1), flat(vm_hi[:, :, :])).then_inc(proj_l, 1)
            split_lo(dve, K(C_QX + 2))
            dve.wait_ge(proj_h, 3)
            less(flat(qx_lo[:, :, :]), bank(2, 2), flat(qx_hi[:, :, :])).then_inc(proj_l, 1)
            split_lo(dve, K(C_U + 2))
            dve.memset(pool_u[:, :, 0:U0], 0.0)
            dve.memset(pool_a[:, :, 0:U0], 0.0)
            link(dve.memset(pool_b[:, :, 0:U0], 0.0))
            after(dve, K(C_U))
            dve.tensor_copy(pool_u[:, :, U0:], bank(4, 2).rearrange("p (c t) -> p c t", c=2)).then_inc(pool_d, 1)
            dve.wait_ge(pool_d, 1)

            def window(dst, src, rows, c, shift):
                link(dve.tensor_tensor(dst[rows, c, U0:], src[rows, c, U0:], src[rows, c, U0 - shift:U0 + S - shift], ALU.add))

            lo_r, hi_r, all_r = slice(0, DH), slice(DH, P), slice(0, P)
            sums = ((0, lo_r, 2), (0, hi_r, 4), (1, lo_r, 8), (1, hi_r, 16))
            window(pool_a, pool_u, all_r, 0, 1)
            window(pool_b, pool_a, hi_r, 0, 2)
            link(dve.tensor_copy(pool_a[hi_r, 0, U0:], pool_b[hi_r, 0, U0:]))
            window(pool_a, pool_u, all_r, 1, 1)
            window(pool_b, pool_a, all_r, 1, 2)
            window(pool_a, pool_b, all_r, 1, 4)
            window(pool_b, pool_a, hi_r, 1, 8)
            link(dve.tensor_copy(pool_a[hi_r, 1, U0:], pool_b[hi_r, 1, U0:]))
            dve.wait_ge(consts_ready, 1)
            for c, r, w in sums:
                link(dve.tensor_scalar(inv_n[r, c, :], pos[r, :], float(w), None, ALU.min))
            link(dve.reciprocal(inv_n[:, :, :], inv_n[:, :, :]))
            for c, r, w in sums:
                link(dve.tensor_tensor(pool_a[r, c, U0:U0 + 16], pool_a[r, c, U0:U0 + 16], inv_n[r, c, :], ALU.mult))
                link(dve.tensor_scalar(pool_a[r, c, U0 + 16:], pool_a[r, c, U0 + 16:], 1.0 / w, None, ALU.mult))
            dve.tensor_tensor(pool_a[:, :, U0:], pool_a[:, :, U0:], pool_u[:, :, U0:], ALU.subtract).then_inc(pool_d, 1)
            def qk_lo(n, b):
                dve.wait_ge(qk_h, n + 1)
                hi, lo = (k_hi, k_lo) if n % 2 else (q_hi, q_lo)
                dve.scalar_tensor_tensor(lo[:, n // 2 % 2, :], bank(b), 1.0 if n % 2 else SCALE,
                                         hi[:, n // 2 % 2, :].bitcast(F32), ALU.mult, ALU.subtract).then_inc(qk_l, 1)

            def cross_max(r):
                dve.wait_ge(xs_ps, r + 1)
                link(dve.tensor_reduce(nmx[:, r, :], bank(4, 4).rearrange("p (i m) -> p i m", m=MEM), AX_X, ALU.max))
                dve.tensor_scalar(nmx[:, r, :], nmx[:, r, :], -SCALE, None, ALU.mult).then_inc(xs_max, 1)

            def cross_norm(r):
                dve.wait_ge(xs_exp, r + 1)
                link(dve.reciprocal(rden[:, r, :], den[:, r, :]))
                for i in range(8):
                    ins = dve.tensor_scalar(probs[:, i, :], probs[:, i, :], rden[:, r, i:i + 1], None, ALU.mult)
                ins.then_inc(xs_norm, 1)

            def cross_t(r):
                dve.wait_ge(xt_h, r + 1)
                less(flat(pT_lo[:, :, :]), bank(4, 4), flat(pT_hi[:, :, :])).then_inc(xt_l, 1)

            def cross_o(r):
                dve.wait_ge(xo_h, r + 1)
                for h in range(2):
                    rows = slice(DH * h, DH * h + DH)
                    ins = less(xaT_lo[rows, r, :], bank(6 * r + h)[rows, :], xaT_hi[rows, r, :])
                ins.then_inc(xo_l, 1)

            cross_max(0)
            cross_norm(0)
            split_lo(dve, K(C_PAIR))
            dve.wait_ge(proj_h, 4)
            less(flat(v_lo[:, :, :]), bank(0, 4), flat(v_hi[:, :, :])).then_inc(proj_l, 1)
            split_lo(dve, K(C_PAIR + 1))
            dve.wait_ge(pool_h, 2)
            for c in range(2):
                dve.scalar_tensor_tensor(plT_lo[:, c, :], bank(c), gains[:, 2 * KD + c:2 * KD + c + 1],
                                         plT_hi[:, c, :].bitcast(F32), ALU.mult, ALU.subtract).then_inc(pool_l, 1)
            cross_t(0)
            qk_lo(0, 2)
            qk_lo(1, 3)
            cross_o(0)
            split_lo(dve, K(C_PAIR + 2))
            cross_max(1)
            cross_norm(1)
            qk_lo(2, 2)
            qk_lo(3, 3)
            split_lo(dve, K(C_PAIR + 3))
            cross_t(1)
            cross_o(1)
            split_lo(dve, K(C_MERGE))

            for n in range(HEADS + 2):
                if n < HEADS:
                    dve.wait_ge(z_ln, n + 1)
                    if n >= 1:
                        dve.wait_ge(tail_ps, n)
                    dve.scalar_tensor_tensor(soft[:, :], bank(3 * (n % 2), 3)[:, 0:ZW], 0.0, log_in[:, :],
                                             ALU.max, ALU.add).then_inc(z_soft, 1)
                if n >= 2:
                    m = n - 2
                    rows = slice(DH * (m % 2), DH * (m % 2) + DH)
                    dve.wait_ge(av_h, m + 1)
                    less(sbT_lo[rows, m // 2, :], bank(7)[rows, :], sbT_hi[rows, m // 2, :]).then_inc(av_l, 1)
                if n < HEADS:
                    dve.wait_ge(soft_h, n + 1)
                    dve.tensor_tensor(soft_lo[:, :], soft[:, :], soft_hi[:, :].bitcast(F32), ALU.subtract).then_inc(soft_l, 1)
                if 1 <= n <= 4:
                    qk_lo(n + 3, 6)
                if 1 <= n <= HEADS:
                    m = n - 1
                    dve.wait_ge(a_exp, m + 1)
                    if m >= 1:
                        dve.wait_ge(av_ps, m)
                    dve.tensor_copy(attn_hi[:, :], attn[m % 2][:, :]).then_inc(a_h, 1)
                    dve.wait_ge(a_h, m + 1)
                    dve.tensor_tensor(attn_lo[m % 2][:, :], attn[m % 2][:, :], attn_hi[:, :].bitcast(F32),
                                      ALU.subtract).then_inc(a_l, 1)
                if n == HEADS - 1:
                    split_lo(dve, K(C_MERGE + 1))

            dve.wait_ge(av_ps, HEADS)
            dve.sem_inc(b_used, 3)
            two = lambda b: bank(b, 2).rearrange("p (c t) -> p c t", c=2)
            with dve.Fori(0, KD // 2) as dp:
                for i in range(PER_DP):
                    split_lo(dve, K(C_MERGE + i + 2, dp, PER_DP), width_of(C_MERGE + (i + 2) % PER_DP))
                    if i >= 3:
                        j = i - 3
                        after(dve, K(C_MERGE + i, dp, PER_DP))
                        if j == 2:
                            dve.wait_ge(b_add, dp + 1)
                        dst = merged if j == 0 else branch
                        dve.tensor_tensor(dst[:, :, :], two(2 * j), sig[:, j, :, :], ALU.mult).then_inc(b_used, 1)
                        if j > 0:
                            dve.wait_ge(b_used, dp * 3 + 3 + j + 1)
                        if j > 0:
                            dve.tensor_tensor(merged[:, :, :], merged[:, :, :], branch[:, :, :], ALU.add) \
                               .then_inc(b_add if j == 1 else mg_ready, 1)
                dve.wait_ge(mg_h, dp + 1)
                dve.tensor_tensor(mgT_lo[:, bass.ds(dp * 2, 2), :], merged[:, :, :],
                                  mgT_hi[:, bass.ds(dp * 2, 2), :].bitcast(F32), ALU.subtract).then_inc(mg_l, 1)
            split_lo(dve, K(C_OUT + 2))
            split_lo(dve, K(C_OUT + 3))
            link(dve.tensor_tensor(before[:, :, :], jm[:, :].unsqueeze(1).broadcast_to([P, NE, NE]),
                                   jm[:, :].unsqueeze(2).broadcast_to([P, NE, NE]), ALU.is_lt))
            link(dve.tensor_scalar(base_c[:, :], e128[:, :], -1.0, float((NE - 1) * P), ALU.mult, ALU.add))
            dve.wait_ge(xres_in, 16)
            after(dve, K(C_OUT + 1))
            dve.tensor_tensor(x2[:, :, 0:512], bank(0, 4).rearrange("p (t n) -> p t n", t=TB),
                              x2[:, :, 0:512], ALU.add).then_inc(x2_half, 1)
            split_lo(dve, K(C_MOE))

            dve.wait_ge(gffn_in, 16)
            dve.wait_ge(x2_half, 1)
            for t in range(TB + 1):
                if t < TB:
                    if t < TB - 1:
                        dve.wait_ge(o_ps, t + 1)
                    else:
                        after(dve, K(C_OUT + 3))
                    dve.tensor_tensor(x2[:, t, 512:1024], bank(4 + t), x2[:, t, 512:1024], ALU.add).then_inc(x2_ready, 1)
                if t >= 1:
                    dve.wait_ge(h2T_ps, t)
                    dve.tensor_copy(h2T[:, t - 1, 4:8, :], bank(2 * ((t - 1) % 2) + 1)).then_inc(h2T_v, 1)
                if t < TB:
                    rsqrt(slice(8 + t, 9 + t), MB + TB + t + 1)
                    dve.scalar_tensor_tensor(h2[:, t, :], x2[:, t, :], rstd[:, 8 + t:9 + t], gffn_bc[:, :],
                                             ALU.mult, ALU.mult).then_inc(h2_ready, 1)
            dve.wait_ge(lg_ps, 1)
            lgw = NG + NE
            for t in range(TB):
                ins = dve.tensor_tensor(lgs[:, t, :], bank(4)[:, t * lgw:(t + 1) * lgw], bias_bc[:, :], ALU.add)
                link(ins)
            gl, el = lgs[:, :, 0:NG], lgs[:, :, NG:lgw]

            def row(v, n):
                return v[:, :].unsqueeze(2).broadcast_to([P, TB, n])

            def each(v, n):
                return v[:, 0:n].unsqueeze(1).broadcast_to([P, TB, n])

            def first_max(dst, vals, mx, lowest, tmp, n):
                link(dve.tensor_reduce(mx[:, :], vals, AX_X, ALU.max))
                link(dve.tensor_tensor(tmp, vals, row(mx, n), ALU.is_equal))
                link(dve.tensor_tensor(tmp, tmp, each(jm, n), ALU.mult))
                link(dve.tensor_reduce(lowest[:, :], tmp, AX_X, ALU.min))
                link(dve.tensor_tensor(dst, each(jm, n), row(lowest, n), ALU.is_equal))

            tmp, gsel, elm = (r[:, :, :] for r in rt[0:3])
            m1, m2 = picked[:, 0, :, :], picked[:, 1, :, :]
            gmax, lowest, v1, v2 = sm[0:4]
            first_max(gsel[:, :, 0:NG], gl, gmax, lowest, tmp[:, :, 0:NG], NG)
            link(dve.tensor_scalar(gsel[:, :, 0:NG], gsel[:, :, 0:NG], 1.0, BIG, ALU.subtract, ALU.mult))
            by_group = lambda v: v.rearrange("p t (g e) -> p t g e", g=NG)
            link(dve.tensor_tensor(by_group(elm), by_group(el),
                                   gsel[:, :, 0:NG].unsqueeze(3).broadcast_to([P, TB, NG, EPG]), ALU.add))
            first_max(m1, elm, v1, lowest, tmp, NE)
            link(dve.scalar_tensor_tensor(elm, m1, -BIG, elm, ALU.mult, ALU.add))
            first_max(m2, elm, v2, lowest, tmp, NE)
            dve.tensor_tensor(onehot_b[:, :, :], m1, m2, ALU.add).then_inc(onehot_ready, 1)
            link(dve.tensor_tensor(ex[:, :, 0:NG], gl, row(gmax, NG), ALU.subtract))
            dve.tensor_tensor(ex[:, :, 4:5], v2[:, :].unsqueeze(2), v1[:, :].unsqueeze(2), ALU.subtract).then_inc(r_max, 1)
            rank = bank(5)[:, 0:TB * NE].rearrange("p (t e) -> p t e", t=TB)
            n_tok = bank(5)[:, TB * NE:(TB + 1) * NE]
            past, slot = (r[:, :, :] for r in rt[5:7])
            extra, obase, base1, incl = (r[:, 0, :] for r in rt[9:13])
            bc = lambda v: v.unsqueeze(1).broadcast_to([P, TB, NE])
            dve.wait_ge(rank_ps, 1)
            dve.tensor_tensor(slot, rank, bc(e128[:, :]), ALU.add)
            link(dve.tensor_scalar(extra, n_tok, float(P), None, ALU.is_gt))
            for m in range(2, TB):
                link(dve.scalar_tensor_tensor(extra, n_tok, float(m * P), extra, ALU.is_gt, ALU.add))
            link(dve.tensor_tensor(ex_before[:, :, :], before[:, :, :],
                                   extra.unsqueeze(1).broadcast_to([P, NE, NE]), ALU.mult))
            link(dve.tensor_reduce(obase, ex_before[:, :, :], AX_X, ALU.add))
            link(dve.scalar_tensor_tensor(base1, obase, float(P), base_c[:, :], ALU.mult, ALU.add))
            link(dve.scalar_tensor_tensor(past, rank, float(P), bc(base1), ALU.is_ge, ALU.mult))
            link(dve.tensor_tensor(slot, slot, past, ALU.add))
            for r, mm in ((0, m1), (1, m2)):
                ins = dve.tensor_tensor(picked_slot[:, r, :, :], mm, slot, ALU.mult)
            link(ins)
            link(dve.tensor_reduce(slot_f[:, :], picked_slot[:, :, :, :].rearrange("p r t e -> p (r t) e"), AX_X, ALU.add))
            link(dve.tensor_copy(slot_i[:, :], slot_f[:, :]))
            dve.tensor_scalar(part_i[:, :].bitcast(U32), slot_i[:, :].bitcast(U32), P - 1, None, ALU.bitwise_and)
            link(dve.tensor_scalar(tile_i[:, :].bitcast(U32), slot_i[:, :].bitcast(U32), 7, None, ALU.logical_shift_right))
            pairs = 2 * TB
            link(dve.tensor_tensor(at_tile[:, :, :], tile_no[:, :].unsqueeze(1).broadcast_to([P, pairs, SLOT_TILES]),
                                   tile_i[:, :].unsqueeze(2).broadcast_to([P, pairs, SLOT_TILES]), ALU.is_equal))
            for dst, part in ((at_block, id_block), (at_row, id_row)):
                dve.tensor_tensor(dst[:, :, :], at_tile[:, :, :],
                                  part[:, :].unsqueeze(2).broadcast_to([P, pairs, SLOT_TILES]), ALU.mult)
            for r in range(2):
                cs = slice(r * TB, (r + 1) * TB)
                dve.tensor_tensor(at_part[:, cs, :], slot_no[:, :].unsqueeze(1).broadcast_to([P, TB, P]),
                                  part_i[:, cs].unsqueeze(2).broadcast_to([P, TB, P]), ALU.is_equal).then_inc(sel_ready, 1)
            dve.wait_ge(rows_ps, 1)
            link(dve.tensor_scalar(y_row[:, :], bank(6)[:, 0:SLOT_TILES], float(NO_ROW), None, ALU.add))
            dve.tensor_scalar(x_row[:, :].bitcast(U32), y_row[:, :].bitcast(U32), 1, None, ALU.logical_shift_right) \
               .then_inc(rows_ready, 1)
            link(dve.tensor_tensor(incl, obase, extra, ALU.add))
            link(dve.tensor_tensor(cmp_t[:, :, :], incl.unsqueeze(1).broadcast_to([P, OVER, NE]),
                                   pos[:, 0:OVER].unsqueeze(2).broadcast_to([P, OVER, NE]), ALU.is_lt))
            link(dve.tensor_reduce(rt[13][:, 0, 1:1 + OVER], cmp_t[:, :, :], AX_X, ALU.add))
            link(dve.tensor_scalar(rt[13][:, 0, 1:1 + OVER], rt[13][:, 0, 1:1 + OVER], float(NE - 1), None, ALU.min))
            link(dve.tensor_copy(rt[13][:, 0, 0:1], incl[:, NE - 1:NE]))
            dve.tensor_copy(tab[:, :], rt[13][:, 0, 0:8]).then_inc(route_ready, 1)
            split_lo(dve, K(C_MOE + 1))
            split_lo(dve, K(C_MOE + 2))
            dve.wait_ge(r_exp, 1)
            link(dve.tensor_reduce(sm[0][:, :], ex[:, :, 0:NG], AX_X, ALU.add))
            e2 = ex[:, :, 4:5].rearrange("p t o -> p (t o)")
            link(dve.tensor_scalar(sm[1][:, :], e2, 1.0, None, ALU.add))
            link(dve.tensor_tensor(sm[0][:, :], sm[0][:, :], sm[1][:, :], ALU.mult))
            link(dve.reciprocal(wts[:, 0, :], sm[0][:, :]))
            link(dve.tensor_tensor(wts[:, 1, :], wts[:, 0, :], e2, ALU.mult))

            def xe_lo(n):
                dve.wait_ge(xe_h, n)
                dve.tensor_tensor(xT_lo[:, :], bank(2, 2), xT_hi[:, :].bitcast(F32), ALU.subtract).then_inc(xe_l, 1)

            def gated(n):
                dve.wait_ge(silu_ready, n)
                dve.tensor_tensor(act_e[:, :], bank(1), silu_g[:, :], ALU.mult).then_inc(act_ready, 1)

            def aT_l(n):
                dve.wait_ge(at_h, n)
                dve.tensor_tensor(aT_lo[:, :], bank(4), aT_hi[:, :].bitcast(F32), ALU.subtract).then_inc(at_l, 1)

            def y_half(c, b, free):
                after(dve, c)
                dve.wait_ge(ye_free, free)
                dve.tensor_copy(ye[b][:, 512:1024], bank(6)).then_inc(y_v, 1)

            xe_lo(1)
            for i in range(1, 4):
                split_lo(dve, K(C_MOE + i + 2))
            gated(1)
            xe_lo(2)
            for i in range(PER_E):
                split_lo(dve, K(C_MOE + 4 + i + 2))
                if i == 1:
                    aT_l(1)
                if i == 3:
                    gated(2)
                    xe_lo(3)
            with dve.Fori(0, NE // 2 - 1) as j:
                for n in range(2):
                    step = dve.snap(j * 2 + n)
                    for i in range(PER_E):
                        split_lo(dve, K(C_MOE + 10 + PER_E * n + i + 2, j, RAW_MOE))
                        if i == 0:
                            y_half(K(C_MOE + 9 + PER_E * n, j, RAW_MOE), n, step + 1)
                        if i == 1:
                            aT_l(step + 2)
                        if i == 3:
                            gated(step + 3)
                            xe_lo(step + 4)
            y_half(K(C_OVER - 3), 0, NE - 1)
            aT_l(NE)
            y_half(K(C_OVER - 1), 1, NE)
            n_over = dve.value_load(tab[0:1, 0:1], min_val=0, max_val=OVER)
            with dve.Fori(0, OVER) as j:
                with dve.If(n_over > j):
                    for i in range(PER_E):
                        split_lo(dve, K(C_OVER + i, j, PER_E))
                    gated(j + NE + 1)
                    xe_lo(j + NE + 2)
                    aT_l(j + NE + 1)
                    y_half(K(C_OVER + 5, j, PER_E), 0, j + NE + 1)
                dve.nop()

            dve.wait_ge(gfin_in, 16)
            for t in range(TB + 1):
                if t < TB:
                    dve.wait_ge(y_back[t], 16)
                    link(dve.scalar_tensor_tensor(x2[:, t, :], y_in[:, t, 0, :], wts[:, 0, t:t + 1], x2[:, t, :],
                                                  ALU.mult, ALU.add))
                    dve.scalar_tensor_tensor(x2[:, t, :], y_in[:, t, 1, :], wts[:, 1, t:t + 1], x2[:, t, :],
                                             ALU.mult, ALU.add).then_inc(comb_ready, 1)
                if t >= 1:
                    u = t - 1
                    rsqrt(slice(12 + u, 13 + u), MB + 2 * TB + u + 1)
                    dve.scalar_tensor_tensor(x2[:, u, :], x2[:, u, :], rstd[:, 12 + u:13 + u], gfin_bc[:, :],
                                             ALU.mult, ALU.mult).then_inc(res_ready, 1)


_INS = ["x", "mem", "norm_mix", "norm_mem", "w_in", "w_pool", "pool_scale", "w_kv_mem", "w_up_sb", "w_up_pool",
        "w_up_x", "w_out", "norm_ffn", "w_group", "b_group", "w_router", "b_router", "w_gate", "w_up", "w_down",
        "norm_final"]


def kernel(**inputs):
    import numpy as np
    import concourse.bacc as bacc
    from concourse.bass_utils import run_bass_kernel_spmd

    nc = bacc.Bacc("TRN2", target_bir_lowering=False, num_devices=1)
    arrays, args = {}, []
    for name in _INS:
        a = np.ascontiguousarray(inputs[name])
        arrays[f"in_{name}"] = a
        args.append(nc.dram_tensor(f"in_{name}", a.shape, mybir.dt.from_np(a.dtype), kind="ExternalInput").ap())
    args.append(nc.dram_tensor("out_0", (1, S, D), F32, kind="ExternalOutput").ap())
    build_trunk(nc, *args)
    r = run_bass_kernel_spmd(nc, [arrays], core_ids=[0])
    return r.results[0]["out_0"]
```
